# Optimizing a Trainium2 kernel written in Bass

```python
import jax, jax.numpy as jnp
from jax import lax
import numpy as np

D_MODEL = 1024
BATCH = 1
SEQ = 512
DEPTH = 2
DEC_BATCH = 8
DEC_SEQ = 1
PAST_LEN = 2048
PAGE_SIZE = 128

N_A_LAYERS = DEPTH // 2
N_B_LAYERS = DEPTH - N_A_LAYERS
CHUNK = 128
SGU_WIDTH = 2 * D_MODEL
SGU_GROUPS = 8
SGU_GROUP_DIM = SGU_WIDTH // SGU_GROUPS
N_HEADS = 8
QK_NOPE = 128
QK_ROPE = 64
V_HEAD = 128
Q_LORA = D_MODEL // 2
KV_LORA = D_MODEL // 4
ROPE_THETA = 10000.0
Q_BLOCK = 128
ATTN_SCALE = (QK_NOPE + QK_ROPE) ** -0.5
D_FF = 11 * D_MODEL // 4
CONV_W = 3
EPS = 1e-6

kernel_name = "yoco_sgu_mla_convffn_step"

def rms_norm(x, g):
    xf = x.astype(jnp.float32)
    y = xf * lax.rsqrt(jnp.mean(xf * xf, axis=-1, keepdims=True) + EPS)
    return (y * g.astype(jnp.float32)).astype(x.dtype)

def rope(x, pos):
    half = QK_ROPE // 2
    inv = 1.0 / (ROPE_THETA ** (jnp.arange(half, dtype=jnp.float32) / half))
    ang = pos.astype(jnp.float32)[:, None] * inv[None, :]
    shp = (ang.shape[0],) + (1,) * (x.ndim - 3) + (half,)
    cos, sin = jnp.cos(ang).reshape(shp), jnp.sin(ang).reshape(shp)
    xf = x.astype(jnp.float32)
    x1, x2 = xf[..., :half], xf[..., half:]
    return jnp.concatenate([x1 * cos - x2 * sin, x2 * cos + x1 * sin], axis=-1).astype(x.dtype)

def sgu_mixer(h, w_in, sgu_g, w_s, b_s, w_out):
    n, t, _ = h.shape
    z = jax.nn.gelu(h @ w_in, approximate=False)
    u, v = jnp.split(z, 2, axis=-1)
    v = rms_norm(v, sgu_g)
    cl = CHUNK if t >= CHUNK else t
    pad = (-t) % cl
    n_chunks = (t + pad) // cl
    vp = jnp.pad(v, ((0, 0), (0, pad), (0, 0))).reshape(n, n_chunks, cl, SGU_GROUPS, SGU_GROUP_DIM)
    causal = jnp.tril(jnp.ones((cl, cl), dtype=bool))
    wm = jnp.where(causal[None], w_s[:, :cl, :cl], 0)
    s = jnp.einsum('gts,ncsgd->nctgd', wm, vp) + b_s[:, :cl].T[:, :, None]
    s = s.reshape(n, n_chunks * cl, SGU_WIDTH)[:, :t]
    return (u * s) @ w_out, v

def conv_ffn(h, conv_prev, w_up, conv_w, conv_b, w_down):
    t = h.shape[1]
    a = h @ w_up
    ap = jnp.concatenate([conv_prev.astype(a.dtype), a], axis=1)
    c = conv_b + ap[:, 0:t] * conv_w[0]
    for k in range(1, CONV_W):
        c = c + ap[:, k:k + t] * conv_w[k]
    g, u = jnp.split(c, 2, axis=-1)
    return (jax.nn.gelu(g, approximate=True) * u) @ w_down, ap[:, t:]

def kv_side(h, pos, kv_in_g, w_dkv, kv_g):
    kv = rms_norm(h, kv_in_g) @ w_dkv
    return rms_norm(kv[..., :KV_LORA], kv_g), rope(kv[..., KV_LORA:], pos)

def mla_attend(q_lat, q_pe, q_pos, ckv, kr, k_pos):
    n, t = q_lat.shape[:2]
    qb = Q_BLOCK if t % Q_BLOCK == 0 else t
    nb = t // qb

    def block(args):
        ql, qp, pq = args
        s = (jnp.einsum('nthc,nsc->nhts', ql, ckv, preferred_element_type=jnp.float32)
             + jnp.einsum('nthr,nsr->nhts', qp, kr, preferred_element_type=jnp.float32)) * ATTN_SCALE
        s = jnp.where(k_pos[None, None, None, :] <= pq[None, None, :, None], s, -jnp.inf)
        p = jax.nn.softmax(s, axis=-1).astype(ckv.dtype)
        return jnp.einsum('nhts,nsc->nthc', p, ckv)

    qlb = q_lat.reshape(n, nb, qb, N_HEADS, KV_LORA).transpose(1, 0, 2, 3, 4)
    qpb = q_pe.reshape(n, nb, qb, N_HEADS, QK_ROPE).transpose(1, 0, 2, 3, 4)
    out = lax.map(block, (qlb, qpb, q_pos.reshape(nb, qb)))
    return out.transpose(1, 0, 2, 3, 4).reshape(n, t, N_HEADS, KV_LORA)

def mla_mixer(h, pos, ckv, kr, k_pos, w_dq, q_g, w_uq, w_uk, w_uv, w_o):
    n, t, _ = h.shape
    cq = rms_norm(h @ w_dq, q_g)
    q = (cq @ w_uq).reshape(n, t, N_HEADS, QK_NOPE + QK_ROPE)
    q_pe = rope(q[..., QK_NOPE:], pos)
    q_lat = jnp.einsum('nthd,chd->nthc', q[..., :QK_NOPE], w_uk)
    o_lat = mla_attend(q_lat, q_pe, pos, ckv, kr, k_pos)
    o = jnp.einsum('nthc,chd->nthd', o_lat, w_uv).reshape(n, t, N_HEADS * V_HEAD)
    return o @ w_o

def run_group(x, pos, past_ckv, past_kr, conv_prev, p):
    v_rows, conv_new = [], []
    ckv_new = kr_new = ckv_all = kr_all = k_pos = None
    for layer in range(DEPTH):
        if layer == N_A_LAYERS:
            ckv_new, kr_new = kv_side(x, pos, p['kv_in_g'], p['w_dkv'], p['kv_g'])
            if past_ckv is None:
                ckv_all, kr_all, k_pos = ckv_new, kr_new, pos
            else:
                past_len = past_ckv.shape[1]
                ckv_all = jnp.concatenate([past_ckv.astype(ckv_new.dtype), ckv_new], axis=1)
                kr_all = jnp.concatenate([past_kr.astype(kr_new.dtype), kr_new], axis=1)
                k_pos = jnp.concatenate([jnp.arange(past_len, dtype=jnp.int32), pos])
        h = rms_norm(x, p['pre_mix_g'][layer])
        if layer < N_A_LAYERS:
            m, v = sgu_mixer(h, p['w_in_a'][layer], p['sgu_g'][layer], p['w_s'][layer],
                             p['b_s'][layer], p['w_out_a'][layer])
            v_rows.append(v)
        else:
            j = layer - N_A_LAYERS
            m = mla_mixer(h, pos, ckv_all, kr_all, k_pos, p['w_dq'][j], p['q_g'][j], p['w_uq'][j],
                          p['w_uk'], p['w_uv'], p['w_o'][j])
        x = x + rms_norm(m, p['post_mix_g'][layer])
        h = rms_norm(x, p['pre_ffn_g'][layer])
        f, cs = conv_ffn(h, conv_prev[layer], p['w_up'][layer], p['conv_w'][layer],
                         p['conv_b'][layer], p['w_down'][layer])
        conv_new.append(cs)
        x = x + rms_norm(f, p['post_ffn_g'][layer])
    return x, ckv_new, kr_new, jnp.stack(conv_new), jnp.stack(v_rows)

def setup_inputs(seed: int = 0) -> dict:
    key = jax.random.key(seed)
    ks = iter(jax.random.split(key, 40))
    f32 = jnp.float32

    def nrm(shape, scale):
        return jax.random.normal(next(ks), shape, f32) * scale

    def gain(shape):
        return 1.0 + 0.1 * jax.random.normal(next(ks), shape, f32)

    n_pages = PAST_LEN // PAGE_SIZE
    n_used = DEC_BATCH * n_pages
    n_pool = n_used + max(1, n_used // 4)
    page_table = jax.random.permutation(next(ks), n_pool)[:n_used].reshape(DEC_BATCH, n_pages).astype(jnp.int32)
    return {
        'x_prompt': nrm((BATCH, SEQ, D_MODEL), 1.0),
        'x_sample': nrm((DEC_BATCH, DEC_SEQ, D_MODEL), 1.0),
        'cache_ckv': nrm((n_pool, PAGE_SIZE, KV_LORA), 1.0),
        'cache_kr': nrm((n_pool, PAGE_SIZE, QK_ROPE), 1.0),
        'state_conv': nrm((DEPTH, DEC_BATCH, CONV_W - 1, 2 * D_FF), 1.0),
        'page_table': page_table,
        'pre_mix_g': gain((DEPTH, D_MODEL)),
        'post_mix_g': gain((DEPTH, D_MODEL)),
        'pre_ffn_g': gain((DEPTH, D_MODEL)),
        'post_ffn_g': gain((DEPTH, D_MODEL)),
        'w_in_a': nrm((N_A_LAYERS, D_MODEL, 2 * SGU_WIDTH), D_MODEL ** -0.5),
        'sgu_g': gain((N_A_LAYERS, SGU_WIDTH)),
        'w_s': nrm((N_A_LAYERS, SGU_GROUPS, CHUNK, CHUNK), CHUNK ** -0.5),
        'b_s': gain((N_A_LAYERS, SGU_GROUPS, CHUNK)),
        'w_out_a': nrm((N_A_LAYERS, SGU_WIDTH, D_MODEL), SGU_WIDTH ** -0.5),
        'kv_in_g': gain((D_MODEL,)),
        'w_dkv': nrm((D_MODEL, KV_LORA + QK_ROPE), D_MODEL ** -0.5),
        'kv_g': gain((KV_LORA,)),
        'w_uk': nrm((KV_LORA, N_HEADS, QK_NOPE), KV_LORA ** -0.5),
        'w_uv': nrm((KV_LORA, N_HEADS, V_HEAD), KV_LORA ** -0.5),
        'w_dq': nrm((N_B_LAYERS, D_MODEL, Q_LORA), D_MODEL ** -0.5),
        'q_g': gain((N_B_LAYERS, Q_LORA)),
        'w_uq': nrm((N_B_LAYERS, Q_LORA, N_HEADS * (QK_NOPE + QK_ROPE)), Q_LORA ** -0.5),
        'w_o': nrm((N_B_LAYERS, N_HEADS * V_HEAD, D_MODEL), (N_HEADS * V_HEAD) ** -0.5),
        'w_up': nrm((DEPTH, D_MODEL, 2 * D_FF), D_MODEL ** -0.5),
        'conv_w': nrm((DEPTH, CONV_W, 2 * D_FF), CONV_W ** -0.5),
        'conv_b': nrm((DEPTH, 2 * D_FF), 0.01),
        'w_down': nrm((DEPTH, D_FF, D_MODEL), D_FF ** -0.5),
    }

def reference(x_prompt, x_sample, cache_ckv, cache_kr, state_conv, page_table,
              pre_mix_g, post_mix_g, pre_ffn_g, post_ffn_g,
              w_in_a, sgu_g, w_s, b_s, w_out_a,
              kv_in_g, w_dkv, kv_g, w_uk, w_uv,
              w_dq, q_g, w_uq, w_o,
              w_up, conv_w, conv_b, w_down):
    p = dict(pre_mix_g=pre_mix_g, post_mix_g=post_mix_g, pre_ffn_g=pre_ffn_g, post_ffn_g=post_ffn_g,
             w_in_a=w_in_a, sgu_g=sgu_g, w_s=w_s, b_s=b_s, w_out_a=w_out_a,
             kv_in_g=kv_in_g, w_dkv=w_dkv, kv_g=kv_g, w_uk=w_uk, w_uv=w_uv,
             w_dq=w_dq, q_g=q_g, w_uq=w_uq, w_o=w_o,
             w_up=w_up, conv_w=conv_w, conv_b=conv_b, w_down=w_down)

    bp, tp, _ = x_prompt.shape
    pos_p = jnp.arange(tp, dtype=jnp.int32)
    conv0 = jnp.zeros((DEPTH, bp, CONV_W - 1, 2 * D_FF), x_prompt.dtype)
    y_prompt, new_ckv_prompt, new_kr_prompt, new_conv_prompt, _ = run_group(
        x_prompt, pos_p, None, None, conv0, p)

    nb, n_pages = page_table.shape
    past_len = n_pages * PAGE_SIZE
    past_ckv = cache_ckv[page_table].reshape(nb, past_len, KV_LORA)
    past_kr = cache_kr[page_table].reshape(nb, past_len, QK_ROPE)
    pos_s = past_len + jnp.arange(x_sample.shape[1], dtype=jnp.int32)
    y_sample, new_ckv_sample, new_kr_sample, new_conv_sample, new_chunkv_sample = run_group(
        x_sample, pos_s, past_ckv, past_kr, state_conv, p)

    return (y_prompt, y_sample, new_ckv_prompt, new_kr_prompt, new_conv_prompt,
            new_ckv_sample, new_kr_sample, new_conv_sample, new_chunkv_sample)


_drawn_inputs = setup_inputs


def setup_inputs(seed=0):
    import zlib

    import numpy as np

    out = dict(_drawn_inputs(seed))
    spreads = {}
    factors = {'conv_b': 4.62}
    for name, (base, spread) in spreads.items():
        noise = np.random.default_rng([zlib.crc32(name.encode()), seed]).standard_normal(out[name].shape)
        drawn = base * np.exp(spread * noise) if base else spread * noise
        out[name] = __import__('jax').numpy.asarray(drawn.astype(out[name].dtype))
    for name, factor in factors.items():
        out[name] = (out[name] * factor).astype(out[name].dtype)
    return out
```

```python
from contextlib import ExitStack

import numpy as np

import concourse.bass as bass
from concourse import mybir

ALU = mybir.AluOpType
ACT = mybir.ActivationFunctionType
F32 = mybir.dt.float32
F32R = mybir.dt.float32r
I32 = mybir.dt.int32
AX_X = mybir.AxisListType.X

P = 128
D = 1024
KD = D // P
SEQ, NS = 512, 8
T = SEQ + NS
HB = T // 2
DEPTH = 2
EPS = 1e-6
GW = 2048
KG = GW // P
GROUPS = 8
DFF = 2816
KF = DFF // P
NF = 2 * KF
H, NOPE, ROPE = 8, 128, 64
QL, CL = 512, 256
KQ, KC = QL // P, CL // P
PAST, PAGE = 2048, 128
NPG = PAST // PAGE
SCALE = float(NOPE + ROPE) ** -0.5
CH = 4
NCH = NPG // CH

U_V, U_U, U_WO = 0, 16, 32
U_UP, U_DN = [48, 145], [92, 189]
U_KV, U_DQ, U_UQ, U_O = 124, 127, 131, 137
U_END = 221
STAGES = 4
DN_SPLIT = [(0, 6), (6, 6), (12, 5), (17, 5)]

G_PREMIX, G_POSTMIX, G_PREFFN, G_POSTFFN = 0, 16, 32, 48
G_SGU, G_KVIN, G_KV, G_Q = 64, 80, 88, 90
C_CB, C_CW = 94, 182
C_ST = C_CW + DEPTH * 3 * NF
C_END = C_ST + DEPTH * NS * 2 * NF
NBLK = (C_END + P - 1) // P

GROUPS_SQ = [("x0", KD, D), ("v", KG, GW), ("m_sgu", KD, D), ("x1", KD, D), ("m_ffn0", KD, D), ("x2", KD, D),
             ("kv", KC, CL), ("cq", KQ, QL), ("m_attn", KD, D), ("x3", KD, D), ("m_ffn1", KD, D)]
GI = {n: i for i, (n, _, _) in enumerate(GROUPS_SQ)}
SQB = {n: sum(c for _, c, _ in GROUPS_SQ[:i]) for i, (n, _, _) in enumerate(GROUPS_SQ)}

CONST_COLS = 4 * P + 2 * T + NS

ROWS = [("pre_mix_g", 16), ("post_mix_g", 16), ("pre_ffn_g", 16), ("post_ffn_g", 16), ("sgu_g", 16), ("kv_in_g", 8),
        ("kv_g", 2), ("q_g", 4), ("conv_b", DEPTH * NF), ("conv_w", DEPTH * 3 * NF), ("state_conv", DEPTH * NS * 2 * NF)]


def pack_pieces():
    pieces, col = [], 0
    for name, rows in ROWS:
        r = 0
        while r < rows:
            n = min(rows - r, P - col % P)
            pieces.append((name, r, col // P, col % P, n))
            r, col = r + n, col + n
    assert col == C_END
    return pieces


def rows_of(ap):
    names = "abcdef"[:len(ap.shape) - 1]
    return ap.rearrange(f"{' '.join(names)} (k z) -> ({' '.join(names)} k) z", z=P)


PACK = pack_pieces()
PACK0 = 16 * sum(p[2] < 4 for p in PACK)
PACK1 = 16 * sum(p[2] >= 4 for p in PACK)


def constants():
    c = np.zeros((P, CONST_COLS), np.float32)
    c[:, 0:P] = np.eye(P, dtype=np.float32)
    half = ROPE // 2
    for m in range(P):
        d = m % ROPE
        c[m + half if d < half else m - half, P + m] = -1.0 if d < half else 1.0
    c[:, 2 * P:3 * P] = np.where(np.arange(P)[None, :] <= np.arange(P)[:, None], 0.0, -1e30)
    inv = np.float32(1.0) / (np.float32(10000.0) ** (np.arange(half, dtype=np.float32) / np.float32(half)))
    pos = np.concatenate([np.arange(SEQ), np.full(NS, PAST)]).astype(np.float32)
    ang = (pos[None, :] * inv[:, None]).astype(np.float32)
    c[:, 3 * P:3 * P + T] = np.tile(np.cos(ang), (4, 1))
    c[:, 3 * P + T:3 * P + 2 * T] = np.tile(np.sin(ang), (4, 1))
    for r in range(NS * H):
        c[r, 3 * P + 2 * T + r // H] = 1.0
    c[:, 3 * P + 2 * T + NS:] = np.arange(P)[:, None] <= np.arange(P)[None, :]
    return c


def dmas_of_unit(n):
    if n == U_KV + 2:
        return 2
    if U_UQ <= n < U_UQ + 4:
        return 2
    if U_UQ + 4 <= n < U_UQ + 6:
        return 4
    return 1


def staged(n):
    return 16 * sum(dmas_of_unit(m) for m in range(n % STAGES, n + 1, STAGES))


def trunk(nc, a, outs):
    ctx = ExitStack()
    with ctx:
        top = [(nc.sbuf_base + 31) // 32 * 32]

        def at(name, shape, offset, dt=F32):
            return nc.alloc_sbuf_tensor_at(name, [P] + shape, dt, offset=offset)

        def size(shape):
            return (4 * int(np.prod(shape)) + 31) // 32 * 32

        def sb(name, shape, dt=F32):
            off = top[0]
            top[0] += size(shape)
            return at(name, shape, off, dt)

        def plan(base, *items):
            out = []
            for name, shape, dt in items:
                out.append(at(name, shape, base, dt))
                base += size(shape)
            assert base <= nc.sbuf_usable_end, (name, base)
            return out + [base]

        x = sb("x", [KD, T])
        xg_base = top[0]
        xh, xl = sb("xh", [KD, T], F32R), sb("xl", [KD, T], F32R)
        ws = sb("ws", [STAGES, 1024])
        wh, wl = sb("wh", [2, 1024], F32R), sb("wl", [2, 1024], F32R)
        pt = sb("pt", [C_END])
        cst = sb("cst", [CONST_COLS])
        ones = sb("ones", [P])
        eps = sb("eps", [1])
        r1, r2 = sb("r1", [T]), sb("r2", [T])
        tmp_base = top[0]
        sq, sqa, ut = sb("sq", [2, T]), sb("sqa", [T]), sb("ut", [2, T])
        arena = top[0]
        ident, perm = cst[:, 0:P], cst[:, P:2 * P]
        cmask = cst[:, 2 * P:3 * P]
        cos, sin = cst[:, 3 * P:3 * P + T], cst[:, 3 * P + T:3 * P + 2 * T]
        own = cst[:, 3 * P + 2 * T:3 * P + 2 * T + NS]
        keep = cst[:, 3 * P + 2 * T + NS:]
        m_raw = at("m_raw", [KD, T], xg_base)

        zv, usl, wmt, bsb, vsn, w00, rn, sT, vn, zs, cvo, wn, pn, gu_end = plan(
            arena, ("zv", [KG, T], F32), ("usl", [KG, T], F32R), ("wmt", [GROUPS, P], F32), ("bsb", [GROUPS, P], F32),
            ("vsn", [KG, NS], F32), ("w00", [GROUPS], F32), ("rn", [CH + 1], F32),
            ("sT", [T], F32), ("vn", [CH, P], F32), ("zs", [T], F32), ("cvo", [CH, P], F32),
            ("wn", [GROUPS, P], F32), ("pn", [NBLK, P], F32))
        ush = at("ush", [KG, T], arena, F32R)
        xn, xs, _ = plan(arena, ("xn", [4, D], F32), ("xs", [D], F32))
        acth, actl, ab, cc, _ = plan(
            arena, ("acth", [KF, T], F32R), ("actl", [KF, T], F32R), ("ab", [2, 2 + SEQ + 3 * NS], F32),
            ("cc", [2, SEQ + 3 * NS], F32))
        cs = at("cs", [2 + NS, NF], tmp_base - size([T]))
        pr, _ = plan(tmp_base + 3 * size([T]), ("pr", [T], F32))
        csn, _ = plan(tmp_base + 3 * size([T]), ("csn", [5, P], F32))
        CW_ = SEQ + 3 * NS
        reg_a = arena
        xkh, xkl, reg_b = plan(reg_a, ("xkh", [KD, T], F32R), ("xkl", [KD, T], F32R))
        kn, v, _ = plan(reg_a, ("kn", [H, SEQ], F32), ("v", [4, D], F32))
        m_attn = at("m_attn", [KD, T], reg_a)
        ckt, krt, uv, qc, qpad, small, pgt, cksn, okn, reg_c = plan(
            reg_b, ("ckt", [KC, T], F32), ("krt", [T], F32), ("uv", [KC, D], F32), ("qc", [3, NS * H], F32),
            ("qpad", [3 * 512 + 64], F32), ("small", [32], F32), ("pgt", [P], I32),
            ("cksn", [320], F32), ("okn", [320], F32))
        pnd, olT, reg_c = plan(reg_c, ("pnd", [NS * H], F32), ("olT", [KC, H, NS], F32))
        cqh, cql, uk, c_end = plan(reg_c, ("cqh", [KQ, T], F32R), ("cql", [KQ, T], F32R), ("uk", [KC, D], F32))
        ukt, _ = plan(reg_c, ("ukt", [H, CL], F32))
        kt, cn, c_end2 = plan(reg_c, ("kt", [2, 3, 512], F32), ("cn", [2, CH, 320], F32))
        pts = at("pts", [NPG, NS * H], reg_c)
        pp, ppt, c_end3 = plan(reg_c, ("pp", [2, SEQ], F32), ("ppt", [2, 4, SEQ], F32))
        reg_f = max(c_end, c_end2, c_end3)
        o, f_end = plan(reg_f, ("o", [H, T], F32))
        kvr, krr, cqr, f_end2 = plan(reg_f, ("kvr", [KC, T], F32), ("krr", [T], F32), ("cqr", [KQ, T], F32))
        assert f_end2 <= f_end
        qn, qrr, qr, _ = plan(xg_base, ("qn", [H, T], F32), ("qrr", [4, T], F32), ("qr", [4, T], F32))
        ps_sb = at("ps_sb", [PAST], xg_base + size([H, T]))
        osn = at("osn", [NS, CL], reg_f)
        yn, _ = plan(arena, ("yn", [5, D], F32))

        psum = ctx.enter_context(nc.psum_tensor("psum", [P, 8, 512], F32))

        def S(name):
            return ctx.enter_context(nc.semaphore(name))

        d_stage = [S(f"d_stage{i}") for i in range(STAGES)]
        d_const, d_pack0, d_pack1, d_xs = S("d_const"), S("d_pack0"), S("d_pack1"), S("d_xs")
        d_x = [S(f"d_x{i}") for i in range(4)]
        d_gate, d_bc, d_out, d_state, cv_sent = (S(n) for n in ("d_gate", "d_bc", "d_out", "d_state", "cv_sent"))
        d_uk, d_pages = S("d_uk"), S("d_pages")
        d_cn = [S(f"d_cn{i}") for i in range(2)]
        w_high, w_low, mm_done = S("w_high"), S("w_low"), S("mm_done")
        sq_done, sq_added, ss_done, ln_done, r_ready = S("sq_done"), S("sq_added"), S("ss_done"), S("ln_done"), S("r_ready")
        x_new, u_mul, xh_ready, xl_ready, xkh_ready, xkl_ready = (S(n) for n in (
            "x_new", "u_mul", "xh_ready", "xl_ready", "xkh_ready", "xkl_ready"))
        xT_done, xin_v, xin_s = S("xT_done"), S("xin_v"), S("xin_s")
        memset_done, packT_done, pack_ready = S("memset_done"), S("packT_done"), S("pack_ready")
        gT_done, wm_ready = S("gT_done"), S("wm_ready")
        evac_sgu, z_done, u_gelu, zs_ready, zT_done, vn_ready = (S(n) for n in (
            "evac_sgu", "z_done", "u_gelu", "zs_ready", "zT_done", "vn_ready"))
        rT_done, rn_ready, mix_done, mix_read, vs_ready, us_prod, ush_ready, usl_ready = (S(n) for n in (
            "rT_done", "rn_ready", "mix_done", "mix_read", "vs_ready", "us_prod", "ush_ready", "usl_ready"))
        vsT_done, cv_ready = S("vsT_done"), S("cv_ready")
        evac_up, state_in, tails, conv_step, conv_done, gelu_done, prod_done, acth_ready, actl_ready = (S(n) for n in (
            "evac_up", "state_in", "tails", "conv_step", "conv_done", "gelu_done", "prod_done", "acth_ready", "actl_ready"))
        csT_done, csn_ready, csn_sent, m_ready = S("csT_done"), S("csn_ready"), S("csn_sent"), S("m_ready")
        evac_kv, evac_dq, evac_uq, rotk_done, rotk_step, ck_step, ckt_ready = (S(n) for n in (
            "evac_kv", "evac_dq", "evac_uq", "rotk_done", "rotk_step", "ck_step", "ckt_ready"))
        cqh_ready, cql_ready, rotq_done, rotq_step = (S(n) for n in (
            "cqh_ready", "cql_ready", "rotq_done", "rotq_step"))
        ukT_done, ukt_ready, ql_done, qpad_ready, qsel_done, sn_done, sn_ready, zpad = (S(n) for n in (
            "ukT_done", "ukt_ready", "ql_done", "qpad_ready", "qsel_done", "sn_done", "sn_ready", "zpad"))
        kv_done, kv_read_a, kv_read_v, nT_done, n_ready, n_sent = (S(n) for n in (
            "kv_done", "kv_read_a", "kv_read_v", "nT_done", "n_ready", "n_sent"))
        cT_done, kt_a, kt_v, sc_done = S("cT_done"), S("kt_a"), S("kt_v"), S("sc_done")
        sm_v, sm_a, pT_done, pts_ready, pnT_done, pnd_ready, pv_done, osn_ready, olT_done, olT_ready, os_done, os_ready = (
            S(n) for n in ("sm_v", "sm_a", "pT_done", "pts_ready", "pnT_done", "pnd_ready", "pv_done", "osn_ready",
                           "olT_done", "olT_ready", "os_done", "os_ready"))
        s_done, s_masked, s_max, s_neg, p_exp, p_rec, p_norm, ppT_done, ppt_ready, ov_done, o_ready = (S(n) for n in (
            "s_done", "s_masked", "s_max", "s_neg", "p_exp", "p_rec", "p_norm", "ppT_done", "ppt_ready", "ov_done", "o_ready"))
        oh_ready, ol_ready, uq_half, pv_last = S("oh_ready"), S("ol_ready"), S("uq_half"), S("pv_last")
        yT_done, y_ready_v, y_ready_a = S("yT_done"), S("y_ready_v"), S("y_ready_a")

        def wait(eng, sem, value):
            if not isinstance(value, int) or value > 0:
                eng.wait_ge(sem, value)

        def f32(ap):
            return ap.bitcast(F32)

        def halves(ap):
            return ap.rearrange("p (h t) -> p h t", h=2)

        def acc(slot):
            return psum[:, 2 * slot:2 * slot + 2, 0:HB]

        def conv_rows(l, k):
            return C_CW + (l * 3 + k) * NF

        POST = [None, G_POSTMIX, G_POSTFFN, G_POSTMIX + KD, G_POSTFFN + KD]
        PRE = [G_PREMIX, G_PREFFN, G_PREMIX + KD, G_PREFFN + KD, None]

        block = ctx.enter_context(nc.Block())

        @block.sync
        def _(sp):
            def free(n):
                wait(sp, w_low, n - (STAGES - 1))

            def put(n, slot, src, k, cols=P, off=0):
                dst = ws[:, slot, off:off + k * cols].rearrange("p (k c) -> p k c", c=cols)
                sp.dma_start(dst, src.rearrange("(k p) c -> p k c", p=P)).then_inc(d_stage[slot], 16)

            sp.dma_start(cst[:, :], a["consts"]).then_inc(d_const, 16)
            for c in range(4):
                sp.dma_start(xn[:, c, :], a["x_prompt"][0, c * P:(c + 1) * P, :]).then_inc(d_x[c], 16)
            sp.dma_start(xs[0:NS, :], a["x_sample"][:, 0, :]).then_inc(d_xs, 16)

            w_in, w_out = a["w_in_a"][0], a["w_out_a"][0]
            for phase, base, col in ((0, U_V, GW), (1, U_U, 0)):
                def v_units(i, base=base, col=col):
                    for u in range(4):
                        n = base + 4 * i + u
                        free(n)
                        put(n, u, w_in[:, bass.ds(col + (4 * i + u) * P, P)], KD)
                if phase == 0:
                    v_units(0)
                with sp.Fori(1 if phase == 0 else 0, 4) as i:
                    v_units(i)
            with sp.Fori(0, 4) as i:
                for u in range(4):
                    n = U_WO + 4 * i + u
                    free(n)
                    put(n, u, w_out[(u % 2) * D:(u % 2 + 1) * D, bass.ds((2 * i + u // 2) * P, P)], KD)

            def mlp(l):
                up, down = a["w_up"][l], a["w_down"][l]
                with sp.Fori(0, NF // 4) as i:
                    for u in range(4):
                        n = U_UP[l] + 4 * i + u
                        free(n)
                        put(n, (U_UP[l] + u) % STAGES, up[:, bass.ds((u % 2) * DFF + (2 * i + u // 2) * P, P)], KD)
                with sp.Fori(0, KD) as i:
                    for u, (k0, k) in enumerate(DN_SPLIT):
                        n = U_DN[l] + 4 * i + u
                        free(n)
                        put(n, (U_DN[l] + u) % STAGES, down[k0 * P:(k0 + k) * P, bass.ds(i * P, P)], k)

            mlp(0)
            w_dkv, w_dq, w_uq, w_o = a["w_dkv"], a["w_dq"][0], a["w_uq"][0], a["w_o"][0]
            for t in range(3):
                n = U_KV + t
                free(n)
                if t < 2:
                    put(n, n % STAGES, w_dkv[:, t * P:(t + 1) * P], KD)
                else:
                    for c in range(2):
                        dst = ws[:, n % STAGES, :].rearrange("p (k c) -> p k c", c=P)[:, :, c * ROPE:(c + 1) * ROPE]
                        sp.dma_start(dst, w_dkv[:, CL:CL + ROPE].rearrange("(k p) c -> p k c", p=P)).then_inc(
                            d_stage[n % STAGES], 16)
            for t in range(KQ):
                n = U_DQ + t
                free(n)
                put(n, n % STAGES, w_dq[:, t * P:(t + 1) * P], KD)
            for j in range(6):
                n = U_UQ + j
                free(n)
                for e in range(2):
                    if j < 4:
                        put(n, n % STAGES, w_uq[:, (2 * j + e) * (NOPE + ROPE):(2 * j + e) * (NOPE + ROPE) + NOPE], KQ, off=e * KQ * P)
                    else:
                        for hh in range(2):
                            col = (4 * (j - 4) + 2 * e + hh) * (NOPE + ROPE) + NOPE
                            dst = ws[:, n % STAGES, e * KQ * P:(e + 1) * KQ * P].rearrange("p (k c) -> p k c", c=P)
                            sp.dma_start(dst[:, :, hh * ROPE:(hh + 1) * ROPE],
                                         w_uq[:, col:col + ROPE].rearrange("(k p) c -> p k c", p=P)).then_inc(
                                d_stage[n % STAGES], 16)
            for t in range(4):
                n = U_O + t
                free(n)
                put(n, n % STAGES, w_o[:, t * P:(t + 1) * P], KD)

            sp.wait_ge(d_pages, 16)
            for g in range(2 * NS * NCH):
                s, c = g % (NS * NCH) // NCH, g % NCH
                if g == 0:
                    sp.wait_ge(kv_done, 8)
                if g >= 2:
                    if g - 2 < NS * NCH:
                        sp.wait_ge(cT_done, g - 1)
                    else:
                        sp.wait_ge(pv_done, g - 1 - NS * NCH)
                for j in range(CH):
                    page = sp.value_load(pgt[0:1, s * NPG + c * CH + j:s * NPG + c * CH + j + 1], min_val=0,
                                         max_val=a["cache_ckv"].shape[0] - 1)
                    sp.dma_start(cn[:, g % 2, j, 0:CL], a["cache_ckv"][bass.ds(page, 1), :, :].rearrange(
                        "o p c -> (o p) c")).then_inc(d_cn[g % 2], 16)
                    if g < NS * NCH:
                        sp.dma_start(cn[:, g % 2, j, CL:CL + ROPE], a["cache_kr"][bass.ds(page, 1), :, :].rearrange(
                            "o p c -> (o p) c")).then_inc(d_cn[g % 2], 16)
            for t in range(4, KD):
                n = U_O + t
                free(n)
                put(n, n % STAGES, w_o[:, t * P:(t + 1) * P], KD)
            mlp(1)

            for c in range(5):
                sp.wait_ge(y_ready_v, c + 1)
                sp.wait_ge(y_ready_a, c + 1)
                if c < 4:
                    sp.dma_start(outs["y_prompt"][0, c * P:(c + 1) * P, :], yn[:, c, :]).then_inc(d_out, 16)
                else:
                    sp.dma_start(outs["y_sample"][:, 0, :], yn[0:NS, c, :]).then_inc(d_out, 16)
            sp.wait_ge(d_out, 16 * 5)

        @block.gpsimd
        def _(pool):
            pool.dma_start(outs["new_conv_sample"][:, :, 0, :], a["state_conv"][:, :, 1, :]).then_inc(d_state, 16)

            def mlp(l):
                def tile(i, u):
                    q = NF * l + 4 * i + u
                    f = (u % 2) * KF + 2 * i + u // 2
                    wait(pool, conv_done, q - 1)
                    st = pt[:, C_ST + l * NS * 2 * NF:C_ST + (l + 1) * NS * 2 * NF].rearrange(
                        "p (s k f) -> p s k f", s=NS, k=2)
                    dst = ab[:, u % 2, 2 + SEQ:].rearrange("p (s k) -> p s k", k=3)
                    pool.tensor_copy(dst[:, :, 0:2], st[:, :, :, bass.ds(f, 1)].rearrange("p s k o -> p s (k o)")).then_inc(state_in, 1)
                    pool.wait_ge(evac_up, q + 1)
                    pool.tensor_copy(cs[:, 0:2, bass.ds(f, 1)].rearrange("p k o -> p (k o)"), ab[:, u % 2, SEQ:SEQ + 2])
                    pool.tensor_copy(cs[:, 2:2 + NS, bass.ds(f, 1)].rearrange("p k o -> p (k o)"), dst[:, :, 2]).then_inc(tails, 1)

                if l == 0:
                    pool.wait_ge(pack_ready, 4)
                    pool.wait_ge(usl_ready, KG)
                else:
                    pool.wait_ge(csT_done, 1)
                    pool.wait_ge(ol_ready, H)
                pool.wait_ge(x_new, KD * (1 + 2 * l))
                pool.memset(ab[:, :, 0:2], 0.0).then_inc(zpad, 1)
                for u in range(4):
                    tile(0, u)
                with pool.Fori(1, NF // 4) as i:
                    for u in range(4):
                        tile(i, u)
                pool.wait_ge(csn_ready, l + 1)
                pool.dma_start(outs["new_conv_prompt"][l, 0].rearrange("k (f c) -> (k f) c", c=P),
                               csn[0:2 * NF, 0, :]).then_inc(csn_sent, 16)
                for g in range(4):
                    for e in range(2):
                        pool.dma_start(outs["new_conv_sample"][l, 2 * g + e, 1].rearrange("(f c) -> f c", c=P),
                                       csn[e * NF:(e + 1) * NF, g + 1, :]).then_inc(csn_sent, 16)

            for g in range(4):
                pool.wait_ge(cv_ready, g + 1)
                pool.dma_start(outs["new_chunkv_sample"][0, :, 0, g * 512:(g + 1) * 512],
                               cvo[0:NS, :, :].rearrange("p a b -> p (a b)")).then_inc(cv_sent, 16)
            mlp(0)
            pool.wait_ge(mm_done, U_DN[0] + 4 * KD)
            pool.dma_start(uk[:, :, :], a["w_uk"].rearrange("(k p) h d -> p k (h d)", p=P)).then_inc(d_uk, 16)
            pool.dma_start(uv[:, :, :], a["w_uv"].rearrange("(k p) h d -> p k (h d)", p=P)).then_inc(d_uk, 16)
            pool.dma_start(pgt[0:1, :], a["page_table"].rearrange("(o s) g -> o (s g)", o=1)).then_inc(d_pages, 16)
            pool.memset(qpad[:, :], 0.0).then_inc(zpad, 1)
            for c in range(5):
                pool.wait_ge(n_ready, c + 1)
                src = okn if c < 4 else cksn
                rows = P if c < 4 else NS
                dst_c = outs["new_ckv_prompt"][0, c * P:(c + 1) * P, :] if c < 4 else outs["new_ckv_sample"][:, 0, :]
                dst_r = outs["new_kr_prompt"][0, c * P:(c + 1) * P, :] if c < 4 else outs["new_kr_sample"][:, 0, :]
                pool.dma_start(dst_c, src[0:rows, 0:CL]).then_inc(n_sent, 16)
                pool.dma_start(dst_r, src[0:rows, CL:CL + ROPE]).then_inc(n_sent, 16)
            mlp(1)
            pool.wait_ge(d_state, 16)
            pool.wait_ge(cv_sent, 16 * 4)
            pool.wait_ge(n_sent, 16 * 10)
            pool.wait_ge(csn_sent, 16 * 9 * DEPTH)

        @block.tensor
        def _(pe):
            def product(n, slot, nslot, k, kk, rh, rl, first, last):
                hw, lw = wh[:, nslot, kk * P:(kk + 1) * P], wl[:, nslot, kk * P:(kk + 1) * P]
                for w, r, st, en in ((hw, rh, first, False), (hw, rl, False, False), (lw, rh, False, last)):
                    for b in range(2):
                        mm = pe.matmul(psum[:, 2 * slot + b, 0:HB], w, r[:, k, b * HB:(b + 1) * HB], start=st, stop=en)
                return mm

            def unit(n, nslot, slot, ks, rh, rl, first, last, ready=None, koff=0):
                pe.wait_ge(w_low, n + 1)
                for kk, k in enumerate(ks):
                    if ready is not None:
                        for sem, v in ready:
                            pe.wait_ge(sem, v + k + 1)
                    mm = product(n, slot, nslot, k, koff + kk, rh, rl, first and kk == 0, last and kk == len(ks) - 1)
                mm.then_inc(mm_done, 1)

            def two_units(n, rh, rl, ready):
                pe.wait_ge(w_low, n + 2)
                for k in range(KD):
                    for sem, v in ready:
                        pe.wait_ge(sem, v + k + 1)
                    for e in range(2):
                        mm = product(n + e, e, (n + e) % 2, k, k, rh, rl, k == 0, k == KD - 1)
                        if k == KD - 1:
                            mm.then_inc(mm_done, 1)

            def rms(name):
                g = GI[name]
                pe.wait_ge(sq_added, SQB[name] + GROUPS_SQ[g][1])
                wait(pe, ln_done, g)
                for b in range(2):
                    mm = pe.matmul(psum[:, 6 + b, 0:HB], ones[:, :], sqa[:, b * HB:(b + 1) * HB], start=True, stop=True)
                mm.then_inc(ss_done, 1)

            pe.wait_ge(d_const, 16)
            pe.wait_ge(memset_done, 1)

            def pack(g):
                for b in range(4 * g, min(4 * g + 4, NBLK)):
                    rows = min(P, C_END - b * P)
                    mm = pe.transpose(psum[:, 4 + g % 2, (b % 4) * P:(b % 4) * P + rows], pn[0:rows, b, :], ident[0:rows, 0:rows])
                mm.then_inc(packT_done, 1)

            pe.wait_ge(d_xs, 16)
            for t in range(KD):
                if t >= 2:
                    pe.wait_ge(xin_v, t - 1)
                    pe.wait_ge(xin_s, t - 1)
                for c in range(4):
                    if t == 0:
                        pe.wait_ge(d_x[c], 16)
                    pe.transpose(psum[:, 2 * (t % 2), c * P:(c + 1) * P], xn[:, c, t * P:(t + 1) * P], ident)
                pe.transpose(psum[:, 2 * (t % 2) + 1, 0:NS], xs[0:NS, t * P:(t + 1) * P], ident[0:NS, 0:NS]).then_inc(xT_done, 1)
                if t == 0:
                    pe.wait_ge(d_pack0, PACK0)
                    pack(0)

            pe.wait_ge(xin_v, KD)
            pe.wait_ge(xin_s, KD)
            two_units(U_V, xh, xl, [(xl_ready, 0)])
            rms("x0")
            for t in range(2, 4):
                pe.wait_ge(evac_sgu, t - 1)
                unit(U_V + t, t % 2, t % 2, range(KD), xh, xl, True, True)
            pe.wait_ge(d_pack1, PACK1)
            for g in range(1, 4):
                wait(pe, pack_ready, g - 1)
                pack(g)
            pe.wait_ge(d_gate, 16)
            pe.wait_ge(ln_done, 1)
            for g in range(GROUPS):
                mm = pe.transpose(psum[:, 6 + g // 4, (g % 4) * P:(g % 4 + 1) * P], wn[:, g, :], ident)
            mm.then_inc(gT_done, 1)
            with pe.Fori(1, 4) as i:
                for u in range(4):
                    t = 4 * i + u
                    pe.wait_ge(evac_sgu, t - 1)
                    unit(U_V + t, u % 2, u % 2, range(KD), xh, xl, True, True)

            def turn_values():
                for c in range(4):
                    mm = pe.transpose(psum[:, 4, c * P:(c + 1) * P], zs[:, c * P:(c + 1) * P], ident)
                mm.then_inc(zT_done, 1)

            def gate_tile(i, u, first=False):
                j = 4 * i + u
                pe.wait_ge(zs_ready, j + 1)
                wait(pe, vn_ready, j)
                if first:
                    pe.wait_ge(pack_ready, 4)
                    pe.wait_ge(wm_ready, 1)
                turn_values()
                pe.wait_ge(evac_sgu, U_U + j - 1)
                unit(U_U + j, u % 2, u % 2, range(KD), xh, xl, True, True)
                if first:
                    rms("v")
                    pe.wait_ge(r_ready, GI["v"] + 1)
                    for c in range(4):
                        mm = pe.transpose(psum[:, 5, c * P:(c + 1) * P], r2[:, c * P:(c + 1) * P], ident)
                    mm.then_inc(rT_done, 1)
                pe.wait_ge(vn_ready, j + 1)
                wait(pe, mix_read, j)
                g = 2 * i + u // 2
                for c in range(4):
                    mm = pe.matmul(psum[:, 5, c * P:(c + 1) * P], vn[:, c, :], wmt[:, bass.ds(g, 1), :].rearrange("p o t -> p (o t)"),
                                   start=True, stop=True)
                mm.then_inc(mix_done, 1)

            gate_tile(0, 0, first=True)
            for u in range(1, 4):
                gate_tile(0, u)
            with pe.Fori(1, 4) as i:
                for u in range(4):
                    gate_tile(i, u)
            pe.wait_ge(vs_ready, KG)
            wait(pe, vn_ready, KG)
            pe.wait_ge(mix_read, KG)
            pe.wait_ge(ln_done, GI["v"] + 1)
            for g in range(4):
                for c in range(4):
                    mm = pe.transpose(psum[0:NS, 4 + g, c * P:(c + 1) * P], vsn[:, 4 * g + c, :], ident)
                mm.then_inc(vsT_done, 1)

            def wo_tile(i, e, first=False):
                t = 2 * i + e
                wait(pe, sq_done, SQB["m_sgu"] + t - 1)
                for half in range(2):
                    unit(U_WO + 2 * t + half, half, e, range(half * KD, (half + 1) * KD), ush, usl, half == 0, half == 1,
                         ready=[(usl_ready, 0)] if first else None)

            pe.wait_ge(evac_sgu, 2 * KG)
            wo_tile(0, 0, first=True)
            wo_tile(0, 1)
            with pe.Fori(1, 4) as i:
                for e in range(2):
                    wo_tile(i, e)
            pe.wait_ge(cv_ready, 4)
            rms("m_sgu")

            def mlp(l):
                p = 1 + 2 * l
                par = U_UP[l] % 2
                pe.wait_ge(sq_done, SQB["m_attn" if l else "m_sgu"] + KD)
                two_units(U_UP[l], xh, xl, [(xl_ready, KD * p)])
                rms("x1" if l == 0 else "x3")

                def up(i, u):
                    q = 4 * i + u
                    pe.wait_ge(evac_up, NF * l + q - 1)
                    unit(U_UP[l] + q, (par + u) % 2, u % 2, range(KD), xh, xl, True, True)

                for u in range(2, 4):
                    up(0, u)
                with pe.Fori(1, NF // 4) as i:
                    for u in range(4):
                        up(i, u)

                g = "m_ffn0" if l == 0 else "m_ffn1"
                pd = U_DN[l] % 2

                def down(i, e, first=False):
                    t = 2 * i + e
                    if not first:
                        pe.wait_ge(sq_done, SQB[g] + t - 1)
                    for w, (k0, kc) in enumerate(DN_SPLIT):
                        unit(U_DN[l] + 4 * t + w, (pd + w) % 2, e, range(k0, k0 + kc), acth, actl, w == 0, w == 3,
                             ready=[(actl_ready, KF * l)] if first else None)

                pe.wait_ge(evac_up, NF * (l + 1))
                down(0, 0, first=True)
                pe.wait_ge(tails, NF * (l + 1))
                for b in range(5):
                    mm = pe.transpose(psum[0:2 * NF, 6 + b // 4, (b % 4) * P:(b % 4 + 1) * P],
                                      cs[:, :, :].rearrange("p k f -> p (k f)")[:, b * 2 * NF:(b + 1) * 2 * NF], ident)
                mm.then_inc(csT_done, 1)
                down(0, 1, first=False)
                with pe.Fori(1, 4) as i:
                    for e in range(2):
                        down(i, e)
                pe.wait_ge(csn_ready, l + 1)
                rms(g)

            mlp(0)

            pe.wait_ge(sq_done, SQB["m_ffn0"] + KD)
            two_units(U_KV, xkh, xkl, [(xkl_ready, 0)])
            rms("x2")
            pe.wait_ge(evac_kv, 1)
            unit(U_KV + 2, (U_KV + 2) % 2, 0, range(KD), xkh, xkl, True, True)
            for t in range(KQ):
                if t == 0:
                    pe.wait_ge(evac_kv, 2)
                elif t == 1:
                    pe.wait_ge(evac_kv, 3)
                else:
                    pe.wait_ge(evac_dq, t - 1)
                unit(U_DQ + t, (U_DQ + t) % 2, (3 + t) % 2, range(KD), xh, xl, True, True, ready=[(xl_ready, 2 * KD)] if t == 0 else None)
                if t == 0:
                    rms("kv")
            pe.wait_ge(evac_kv, 3)
            for b in range(2):
                mm = pe.matmul(psum[:, 4 + b, 0:HB], perm, krr[:, b * HB:(b + 1) * HB], start=True, stop=True)
            mm.then_inc(rotk_done, 1)
            rms("cq")
            for t in range(12):
                n = U_UQ + t // 2
                if t == 0:
                    pe.wait_ge(evac_dq, 3)
                elif t == 1:
                    pe.wait_ge(evac_dq, 4)
                else:
                    pe.wait_ge(evac_uq, t - 1)
                slot = (7 + t) % 2
                pe.wait_ge(w_low, n + 1)
                for k in range(KQ):
                    if t == 0:
                        pe.wait_ge(cql_ready, k + 1)
                    mm = product(n, slot, n % 2, k, (t % 2) * KQ + k, cqh, cql, k == 0, k == KQ - 1)
                if t % 2:
                    mm.then_inc(mm_done, 1)
                else:
                    mm.then_inc(uq_half, 1)
            for t in range(4):
                pe.wait_ge(evac_uq, 9 + t)
                if t >= 2:
                    pe.wait_ge(rotq_step, 2 * t - 2)
                else:
                    pe.wait_ge(evac_uq, 11 + t)
                slot = (7 + t) % 2
                for b in range(2):
                    mm = pe.matmul(psum[:, 2 * slot + b, 0:HB], perm, qrr[:, t, b * HB:(b + 1) * HB], start=True, stop=True)
                mm.then_inc(rotq_done, 1)

            pe.wait_ge(d_uk, 32)
            pe.wait_ge(rotk_step, 2)
            pe.wait_ge(ln_done, GI["cq"] + 1)
            for h in range(H):
                for c in range(KC):
                    mm = pe.transpose(psum[:, 4 + h // 2, (h % 2) * CL + c * P:(h % 2) * CL + (c + 1) * P], uk[:, c, h * P:(h + 1) * P], ident)
                if h % 2:
                    mm.then_inc(ukT_done, 1)
            pe.wait_ge(rotq_step, 8)
            pe.wait_ge(ukt_ready, 4)
            for c in range(KC):
                for h in range(H):
                    mm = pe.matmul(psum[:, 0, (c * H + h) * NS:(c * H + h + 1) * NS], ukt[:, h, c * P:(c + 1) * P], qn[:, h, SEQ:T],
                                   start=True, stop=True)
            mm.then_inc(ql_done, 1)
            for e in range(2):
                mm = pe.matmul(psum[0:ROPE, 1, e * 32:(e + 1) * 32], ident[:, e * ROPE:(e + 1) * ROPE], qr[:, :, SEQ:T],
                               start=True, stop=True)
            mm.then_inc(qsel_done, 1)
            pe.wait_ge(qpad_ready, 3)
            pe.wait_ge(ckt_ready, KC)
            for c in range(3):
                rows = P if c < 2 else ROPE
                r = ckt[:, c, SEQ:T] if c < 2 else krt[0:ROPE, SEQ:T]
                mm = pe.matmul(psum[0:NS * H, 2, 0:NS], qc[0:rows, c, :], r, start=(c == 0), stop=(c == 2))
            mm.then_inc(sn_done, 1)

            for g in range(16):
                bank = 4 + g % 4
                if g < 4:
                    pe.wait_ge(ukt_ready, 4)
                elif g % 2:
                    pe.wait_ge(kv_read_a, (g - 4) // 2 + 1)
                else:
                    pe.wait_ge(kv_read_v, (g - 4) // 2 + 1)
                for c in range(KC):
                    if g < 8:
                        lw, r = uk[:, c, g * P:(g + 1) * P], ckt[:, c, 0:SEQ]
                    else:
                        tk, hf = (g - 8) // 2, g % 2
                        lw, r = ckt[:, c, tk * P:(tk + 1) * P], uv[:, c, hf * 512:(hf + 1) * 512]
                    mm = pe.matmul(psum[:, bank, :], lw, r, start=(c == 0), stop=(c == KC - 1))
                mm.then_inc(kv_done, 1)
            for c in range(5):
                cols = P if c < 4 else NS
                if c == 0:
                    pe.wait_ge(kv_read_v, 7)
                elif c == 1:
                    pe.wait_ge(kv_read_a, 7)
                else:
                    pe.wait_ge(n_ready, c - 1)
                for k in range(KC):
                    pe.transpose(psum[0:cols, 4 + c % 2, k * P:(k + 1) * P], ckt[:, k, c * P:c * P + cols], ident)
                pe.transpose(psum[0:cols, 4 + c % 2, CL:CL + ROPE], krt[0:ROPE, c * P:c * P + cols], ident[0:ROPE, 0:ROPE]).then_inc(nT_done, 1)

            pe.wait_ge(sn_ready, 1)
            pe.wait_ge(kv_read_v, 8)
            pe.wait_ge(kv_read_a, 8)
            pe.wait_ge(n_ready, 5)

            def turn_chunk(g):
                pe.wait_ge(d_cn[g % 2], 16 * 2 * CH * (g // 2 + 1))
                if g:
                    pe.wait_ge(kt_a, 2 * g)
                    pe.wait_ge(kt_v, g)
                for j in range(CH):
                    for k in range(3):
                        w = P if k < 2 else ROPE
                        mm = pe.transpose(psum[0:w, 4 + k, j * P:(j + 1) * P], cn[:, g % 2, j, k * P:k * P + w], ident)
                mm.then_inc(cT_done, 1)

            def score_chunk(g):
                s, c = g // NCH, g % NCH
                pe.wait_ge(kt_a, 2 * g + 2)
                pe.wait_ge(kt_v, g + 1)
                for k in range(3):
                    rows = P if k < 2 else ROPE
                    mm = pe.matmul(psum[0:NS * H, c, :], qpad[0:rows, k * 512 + s * NS * H:k * 512 + (s + 1) * NS * H],
                                   kt[0:rows, g % 2, k, :], start=(s == 0 and k == 0), stop=(s == NS - 1 and k == 2))
                mm.then_inc(sc_done, 1)

            for g in range(NS * NCH + 1):
                if g < NS * NCH:
                    turn_chunk(g)
                if g:
                    score_chunk(g - 1)
            pe.wait_ge(sm_v, 6)
            for b in range(NPG):
                mm = pe.transpose(psum[:, 4 + b // 8, (b % 8) * 64:(b % 8) * 64 + 64], ps_sb[0:NS * H, b * P:(b + 1) * P], ident[0:64, 0:64])
            mm.then_inc(pT_done, 1)
            pe.transpose(psum[0:NS, 6, 0:NS * H], small[0:NS * H, 16:24], ident[0:64, 0:64]).then_inc(pnT_done, 1)
            pe.wait_ge(pts_ready, 2)
            pe.wait_ge(pnd_ready, 1)
            for g in range(NS * NCH):
                s, c = g // NCH, g % NCH
                gg = NS * NCH + g
                pe.wait_ge(d_cn[gg % 2], 16 * (2 * CH * (NS * NCH // 2) + CH * (g // 2 + 1)))
                for j in range(CH):
                    mm = pe.matmul(psum[0:H, s // 2, (s % 2) * CL:(s % 2 + 1) * CL], pts[:, c * CH + j, s * H:(s + 1) * H],
                                   cn[:, gg % 2, j, 0:CL], start=(c == 0 and j == 0), stop=False)
                mm.then_inc(pv_done, 1)
                if c == NCH - 1:
                    mm = pe.matmul(psum[0:H, s // 2, (s % 2) * CL:(s % 2 + 1) * CL], pnd[0:NS, s * H:(s + 1) * H], cksn[0:NS, 0:CL],
                                   start=False, stop=True)
            mm.then_inc(pv_last, 1)
            pe.wait_ge(osn_ready, 1)
            for c in range(KC):
                for s in range(NS):
                    mm = pe.transpose(psum[:, 4, (c * NS + s) * H:(c * NS + s + 1) * H], osn[0:H, s, c * P:(c + 1) * P], ident[0:H, 0:H])
            mm.then_inc(olT_done, 1)
            pe.wait_ge(olT_ready, 1)
            for h in range(H):
                for c in range(KC):
                    mm = pe.matmul(psum[:, 5, h * NS:(h + 1) * NS], uv[:, c, h * P:(h + 1) * P], olT[:, c, h, :],
                                   start=(c == 0), stop=(c == KC - 1))
            mm.then_inc(os_done, 1)

            pe.wait_ge(os_ready, 1)
            pe.wait_ge(osn_ready, 1)

            def scores(g):
                h, b = g // 4, g % 4
                if g >= 4:
                    pe.wait_ge(p_exp, g - 3)
                n = (b + 1) * P
                lo = (h % 2) * ROPE
                pe.matmul(psum[:, g % 4, 0:n], qn[:, h, b * P:(b + 1) * P], kn[:, h, 0:n], start=True, stop=False)
                pe.matmul(psum[:, g % 4, 0:n], qr[lo:lo + ROPE, h // 2, b * P:(b + 1) * P], krt[lo:lo + ROPE, 0:n],
                          start=False, stop=True).then_inc(s_done, 1)

            def turn_probs(g):
                h, b = g // 4, g % 4
                pe.wait_ge(p_norm, g + 1)
                if g >= 2:
                    pe.wait_ge(ppt_ready, g - 1)
                for j in range(b + 1):
                    mm = pe.transpose(psum[:, 4 + g % 2, j * P:(j + 1) * P], pp[:, g % 2, j * P:(j + 1) * P], ident)
                mm.then_inc(ppT_done, 1)

            def values(h):
                pe.wait_ge(ppt_ready, 4 * h + 4)
                if h >= 2:
                    pe.wait_ge(o_ready, h - 1)
                for j in range(4):
                    mm = pe.matmul(psum[:, 6 + h % 2, j * P:SEQ], v[:, j, h * P:(h + 1) * P], ppt[:, h % 2, j, j * P:SEQ],
                                   start=(j == 0), stop=(j == 3))
                mm.then_inc(ov_done, 1)

            for g in range(4 * H + 3):
                if g < 4 * H:
                    scores(g)
                if 2 <= g < 4 * H + 2:
                    turn_probs(g - 2)
                if g >= 6 and (g - 6) % 4 == 0:
                    values((g - 6) // 4)

            pe.wait_ge(p_exp, 4 * H)
            for t in range(KD):
                if t >= 2:
                    pe.wait_ge(sq_done, SQB["m_attn"] + t - 1)
                unit(U_O + t, (U_O + t) % 2, t % 2, range(KD), xh, xl, True, True, ready=[(ol_ready, 0)] if t == 0 else None)
            pe.wait_ge(o_ready, H)
            rms("m_attn")

            mlp(1)

            for c in range(5):
                cols = P if c < 4 else NS
                if c == 0:
                    pe.wait_ge(x_new, 4 * KD)
                if c >= 2:
                    pe.wait_ge(y_ready_v, c - 1)
                    pe.wait_ge(y_ready_a, c - 1)
                for t in range(KD):
                    mm = pe.transpose(psum[0:cols, 2 * (c % 2) + t // 4, (t % 4) * P:(t % 4 + 1) * P], x[:, t, c * P:c * P + cols], ident)
                mm.then_inc(yT_done, 1)

        @block.scalar
        def _(act):
            def fixed_wait():
                act.wait_ge(memset_done, 1)

            def split(n, slot4, slot2, stage_value):
                act.wait_ge(d_stage[slot4], stage_value)
                wait(act, mm_done, n - 1)
                act.activation(wh[:, slot2, :], ws[:, slot4, :], ACT.Copy).then_inc(w_high, 1)

            def ahead(base, per, i, u):
                m = base + u + 2
                n = m + per * i
                split(n, m % STAGES, m % 2, staged(m) + 16 * (per // STAGES) * i)

            def ahead_static(n):
                if n + 2 < U_END:
                    split(n + 2, (n + 2) % STAGES, n % 2, staged(n + 2))

            def rms(name, dst):
                g = GI[name]
                act.wait_ge(ss_done, g + 1)
                act.activation(halves(dst[:, :]), psum[:, 6:8, 0:HB], ACT.Ln, bias=eps[:, 0:1], scale=1.0 / GROUPS_SQ[g][2]).then_inc(ln_done, 1)
                act.wait_ge(ln_done, g + 1)
                act.activation(dst[:, :], dst[:, :], ACT.Exp, scale=-0.5).then_inc(r_ready, 1)

            def square(src, name, t, slot):
                wait(act, sq_added, SQB[name] + t - 1)
                out = sq[:, slot, :]
                act.activation(halves(out) if len(src.shape) == 3 else out, src, ACT.Square).then_inc(sq_done, 1)

            def update(p):
                name = f"x{p}"
                for t in range(KD):
                    if p:
                        act.wait_ge(x_new, KD * (p - 1) + t + 1)
                    else:
                        act.wait_ge(xin_v, t + 1)
                        act.wait_ge(xin_s, t + 1)
                        if t == 0:
                            act.wait_ge(pack_ready, 1)
                    if p == 2:
                        act.activation(xkh[:, t, :], x[:, t, :], ACT.Copy, scale=pt[:, G_KVIN + t:G_KVIN + t + 1]).then_inc(xkh_ready, 1)
                    else:
                        act.activation(xh[:, t, :], x[:, t, :], ACT.Copy, scale=pt[:, PRE[p] + t:PRE[p] + t + 1]).then_inc(xh_ready, 1)
                    square(x[:, t, :], name, t, t % 2)
                if p == 2:
                    for t in range(KD):
                        act.activation(xh[:, t, :], x[:, t, :], ACT.Copy, scale=pt[:, PRE[p] + t:PRE[p] + t + 1]).then_inc(xh_ready, 1)

            def raw(name, t, slot, m_dst):
                fixed_wait()
                act.activation(halves(m_dst), acc(slot), ACT.Copy).then_inc(m_ready, 1)
                square(acc(slot), name, t, slot % 2)

            for k, (src, r0, b, lo, n) in enumerate(PACK):
                act.dma_start(pn[lo:lo + n, b, :], rows_of(a[src] if len(a[src].shape) > 1 else a[src].rearrange("(o k) -> o k", o=1))[r0:r0 + n, :]).then_inc(
                    d_pack0 if b < 4 else d_pack1, 16)
            act.dma_start(wn[:, :, :], a["w_s"][0].rearrange("g t s -> t g s")).then_inc(d_gate, 16)
            act.dma_start(bsb[:, :, :], a["b_s"][0].partition_broadcast(P)).then_inc(d_bc, 16)
            act.dma_start(w00[:, :], a["w_s"][0, :, 0, 0].partition_broadcast(P), allow_slow_non_contiguous=True).then_inc(d_bc, 16)

            act.wait_ge(packT_done, 1)
            act.activation(pt[:, 0:512], psum[:, 4, :], ACT.Copy).then_inc(pack_ready, 1)
            for t in range(KD):
                act.wait_ge(xT_done, t + 1)
                act.activation(x[:, t, SEQ:T], psum[:, 2 * (t % 2) + 1, 0:NS], ACT.Copy).then_inc(xin_s, 1)
            split(0, 0, 0, staged(0))
            split(1, 1, 1, staged(1))
            update(0)

            def value_tile(i, u):
                j = 4 * i + u
                wait(act, sq_added, SQB["v"] + j - 1)
                act.wait_ge(evac_sgu, j + 1)
                fixed_wait()
                act.activation(zv[:, bass.ds(j, 1), :].rearrange("p o t -> p (o t)"), ut[:, u % 2, :], ACT.Gelu).then_inc(z_done, 1)
                fixed_wait()
                act.wait_ge(z_done, j + 1)
                act.activation(sq[:, u % 2, :], zv[:, bass.ds(j, 1), :].rearrange("p o t -> p (o t)"), ACT.Square).then_inc(sq_done, 1)

            for u in range(4):
                ahead(U_V, 4, 0, u)
                if u == 0:
                    rms("x0", r1)
                value_tile(0, u)
            for g in range(1, 4):
                act.wait_ge(packT_done, g + 1)
                n = min(512, C_END - 512 * g)
                act.activation(pt[:, 512 * g:512 * g + n], psum[:, 4 + g % 2, 0:n], ACT.Copy).then_inc(pack_ready, 1)
            with act.Fori(1, 4) as i:
                for u in range(4):
                    ahead(U_V, 4, i, u)
                    value_tile(i, u)

            def gate_tile(i, u, first=False):
                j = 4 * i + u
                if first:
                    ahead(U_U, 4, i, u)
                    rms("v", r2)
                    act.wait_ge(rT_done, 1)
                    act.activation(rn[:, 0:4], psum[:, 5, :].rearrange("p (c t) -> p c t", c=4)[:, :, 0], ACT.Copy).then_inc(rn_ready, 1)
                    act.wait_ge(rn_ready, 1)
                act.wait_ge(zT_done, j + 1)
                wait(act, mix_done, j)
                for c in range(4):
                    mm = act.activation(vn[:, c, :], psum[:, 4, c * P:(c + 1) * P], ACT.Copy, scale=rn[:, c:c + 1])
                mm.then_inc(vn_ready, 1)
                if not first:
                    ahead(U_U, 4, i, u)
                act.wait_ge(evac_sgu, KG + j + 1)
                wait(act, us_prod, j)
                act.activation(ut[:, 1, :], ut[:, 0, :], ACT.Gelu).then_inc(u_gelu, 1)
                act.wait_ge(us_prod, j + 1)
                fixed_wait()
                act.activation(ush[:, bass.ds(j, 1), :].rearrange("p o t -> p (o t)"), sq[:, 0, :], ACT.Copy).then_inc(ush_ready, 1)

            gate_tile(0, 0, first=True)
            for u in range(1, 4):
                gate_tile(0, u)
            with act.Fori(1, 4) as i:
                for u in range(4):
                    gate_tile(i, u)

            def wo(i):
                for e in range(2):
                    for half in range(2):
                        ahead(U_WO, 4, i, 2 * e + half)
                    t = 2 * i + e
                    act.wait_ge(mm_done, U_WO + 2 * t + 2)
                    raw("m_sgu", t, e, m_raw[:, bass.ds(t, 1), :].rearrange("p o t -> p (o t)"))
            with act.Fori(0, 4) as i:
                wo(i)
            rms("m_sgu", r2)
            update(1)

            def mlp(l):
                def tile(i, u, first=False):
                    ahead(U_UP[l], 4, i, u)
                    if first:
                        rms("x1" if l == 0 else "x3", r1)
                    q, j = 4 * i + u, 2 * i + u // 2
                    if u % 2 == 0:
                        act.wait_ge(conv_done, NF * l + q + 1)
                        act.activation(cc[:, 0, :], cc[:, 0, :], ACT.Gelu_apprx_tanh).then_inc(gelu_done, 1)
                    else:
                        act.wait_ge(prod_done, KF * l + j + 1)
                        fixed_wait()
                        act.activation(acth[:, bass.ds(j, 1), :].rearrange("p o t -> p (o t)"), pr[:, :], ACT.Copy).then_inc(acth_ready, 1)

                for u in range(4):
                    tile(0, u, first=(u == 0))
                with act.Fori(1, NF // 4) as i:
                    for u in range(4):
                        tile(i, u)

                g = "m_ffn0" if l == 0 else "m_ffn1"

                def down(i, e, guard=False):
                    t = 2 * i + e
                    for w in range(4):
                        if guard:
                            ahead_static(U_DN[l] + 4 * t + w)
                        else:
                            ahead(U_DN[l], 8, i, 4 * e + w)
                    act.wait_ge(mm_done, U_DN[l] + 4 * t + 4)
                    raw(g, t, e, m_raw[:, bass.ds(t, 1), :].rearrange("p o t -> p (o t)") if not isinstance(t, int) else m_raw[:, t, :])

                down(0, 0)
                act.wait_ge(csT_done, l + 1)
                act.activation(csn[0:2 * NF, 0:4, :].rearrange("p a b -> p (a b)"), psum[0:2 * NF, 6, :], ACT.Copy)
                act.activation(csn[0:2 * NF, 4, :], psum[0:2 * NF, 7, 0:P], ACT.Copy).then_inc(csn_ready, 1)
                down(0, 1)
                with act.Fori(1, 3) as i:
                    for e in range(2):
                        down(i, e)
                for e in range(2):
                    down(3, e, guard=True)
                rms(g, r2)

            mlp(0)
            update(2)

            ahead_static(U_KV)
            rms("x2", r1)
            for t in range(KC):
                act.wait_ge(evac_kv, t + 1)
                square(kvr[:, t, :], "kv", t, t % 2)
            ahead_static(U_KV + 1)
            ahead_static(U_KV + 2)
            ahead_static(U_DQ)
            rms("kv", r2)
            for t in range(KQ):
                act.wait_ge(evac_dq, t + 1)
                square(cqr[:, t, :], "cq", t, t % 2)
                act.activation(cqh[:, t, :], cqr[:, t, :], ACT.Copy, scale=pt[:, G_Q + t:G_Q + t + 1]).then_inc(cqh_ready, 1)
                if t < KQ - 1:
                    ahead_static(U_DQ + t + 1)
            act.wait_ge(ckt_ready, KC)
            rms("cq", r2)
            for j in range(6):
                ahead_static(U_UQ + j)
            act.wait_ge(d_uk, 32)
            for g in range(4):
                act.wait_ge(ukT_done, g + 1)
                if g == 0:
                    act.wait_ge(mm_done, U_UQ + 6)
                act.activation(ukt[:, 2 * g:2 * g + 2, :].rearrange("p a b -> p (a b)"), psum[:, 4 + g, :], ACT.Copy).then_inc(ukt_ready, 1)
            for g in range(1, 16, 2):
                act.wait_ge(kv_done, g + 1)
                dst = kn[:, g, :] if g < 8 else v[:, (g - 8) // 2, 512:1024]
                act.activation(dst, psum[:, 4 + g % 4, :], ACT.Copy).then_inc(kv_read_a, 1)
            for c in range(5):
                rows = P if c < 4 else NS
                act.wait_ge(nT_done, c + 1)
                if 1 <= c < 4:
                    act.wait_ge(n_sent, 32 * c)
                act.activation((okn if c < 4 else cksn)[0:rows, :], psum[0:rows, 4 + c % 2, 0:320], ACT.Copy).then_inc(n_ready, 1)

            for g in range(NS * NCH):
                act.wait_ge(cT_done, g + 1)
                if g >= 2:
                    act.wait_ge(sc_done, g - 1)
                act.activation(kt[:, g % 2, 0, :], psum[:, 4, :], ACT.Copy).then_inc(kt_a, 1)
                act.activation(kt[0:ROPE, g % 2, 2, :], psum[0:ROPE, 6, :], ACT.Copy).then_inc(kt_a, 1)
            act.wait_ge(sm_v, 3)
            act.activation(ps_sb[0:64, :], psum[0:64, 0:4, :].rearrange("p a b -> p (a b)"), ACT.Exp, bias=small[0:64, 2:3], scale=SCALE,
                           accum_out=small[0:64, 3:4]).then_inc(sm_a, 1)
            act.activation(small[0:64, 4:5], small[0:64, 1:2], ACT.Exp, bias=small[0:64, 2:3], scale=SCALE).then_inc(sm_a, 1)
            act.wait_ge(pT_done, 1)
            act.activation(pts[:, 0:8, :].rearrange("p a b -> p (a b)"), psum[:, 4, :], ACT.Copy).then_inc(pts_ready, 1)
            act.activation(pts[:, 8:16, :].rearrange("p a b -> p (a b)"), psum[:, 5, :], ACT.Copy).then_inc(pts_ready, 1)
            act.wait_ge(pv_last, 1)
            act.activation(osn[0:H, :, :].rearrange("p a b -> p (a b)"), psum[0:H, 0:4, :].rearrange("p a b -> p (a b)"), ACT.Copy).then_inc(osn_ready, 1)

            def turned(g):
                h, b = g // 4, g % 4
                act.wait_ge(ppT_done, g + 1)
                wait(act, ov_done, h - 1)
                act.activation(ppt[:, h % 2, 0:b + 1, b * P:(b + 1) * P], psum[:, 4 + g % 2, 0:(b + 1) * P].rearrange("p (j t) -> p j t", t=P),
                               ACT.Copy).then_inc(ppt_ready, 1)

            for g in range(4 * H):
                b = g % 4
                n = (b + 1) * P
                act.wait_ge(s_neg, g + 1)
                if g >= 2:
                    act.wait_ge(ppT_done, g - 1)
                act.activation(pp[:, g % 2, 0:n], psum[:, g % 4, 0:n], ACT.Exp, bias=small[:, 8 + g % 2:9 + g % 2], scale=SCALE,
                               accum_out=small[:, 10 + g % 2:11 + g % 2]).then_inc(p_exp, 1)
                if g >= 2:
                    turned(g - 2)
            turned(4 * H - 2)
            turned(4 * H - 1)
            for h in range(H):
                act.wait_ge(o_ready, h + 1)
                if h == 0:
                    act.wait_ge(s_done, 4 * H)
                    act.wait_ge(os_ready, 1)
                act.activation(xh[:, h, :], o[:, h, :], ACT.Copy).then_inc(oh_ready, 1)
            for t in range(KD):
                ahead_static(U_O + t)
                act.wait_ge(mm_done, U_O + t + 1)
                raw("m_attn", t, t % 2, m_attn[:, t, :])
            rms("m_attn", r2)
            update(3)
            mlp(1)
            for c in range(5):
                rows = P if c < 4 else NS
                act.wait_ge(yT_done, c + 1)
                act.activation(yn[0:rows, c, 512:1024], psum[0:rows, 2 * (c % 2) + 1, :], ACT.Copy).then_inc(y_ready_a, 1)

        @block.vector
        def _(dve):
            def split(n, slot4, slot2):
                dve.wait_ge(w_high, n + 1)
                dve.tensor_tensor(wl[:, slot2, :], ws[:, slot4, :], f32(wh[:, slot2, :]), ALU.subtract).then_inc(w_low, 1)

            def ahead(base, per, i, u):
                m = base + u + 2
                split(m + per * i, m % STAGES, m % 2)

            def ahead_static(n):
                if n + 2 < U_END:
                    split(n + 2, (n + 2) % STAGES, n % 2)

            def add_squares(name, t, slot, first):
                n = SQB[name] + t
                dve.wait_ge(sq_done, n + 1)
                wait(dve, sq_added, n)
                if first:
                    wait(dve, ss_done, GI[name])
                    dve.tensor_copy(sqa[:, :], sq[:, slot, :]).then_inc(sq_added, 1)
                else:
                    dve.tensor_tensor(sqa[:, :], sqa[:, :], sq[:, slot, :], ALU.add).then_inc(sq_added, 1)

            def low(p, t):
                if p == 2:
                    dve.wait_ge(xkh_ready, t + 1)
                    dve.scalar_tensor_tensor(out=xkl[:, t, :], in0=x[:, t, :], scalar=pt[:, G_KVIN + t:G_KVIN + t + 1], in1=f32(xkh[:, t, :]),
                                             op0=ALU.mult, op1=ALU.subtract).then_inc(xkl_ready, 1)
                else:
                    low_mix(p, t)

            def low_mix(p, t):
                dve.wait_ge(xh_ready, KD * p + t + 1)
                dve.scalar_tensor_tensor(out=xl[:, t, :], in0=x[:, t, :], scalar=pt[:, PRE[p] + t:PRE[p] + t + 1], in1=f32(xh[:, t, :]),
                                         op0=ALU.mult, op1=ALU.subtract).then_inc(xl_ready, 1)

            def update(p, m):
                dve.wait_ge(r_ready, GI[["", "m_sgu", "m_ffn0", "m_attn", "m_ffn1"][p]] + 1)
                if p % 2 == 0:
                    dve.wait_ge(csn_sent, 16 * 9 * (p // 2))
                for t in range(KD):
                    k = KD * (p - 1) + t
                    wait(dve, x_new, k - 1)
                    dve.scalar_tensor_tensor(out=ut[:, t % 2, :], in0=m[:, t, :], scalar=pt[:, POST[p] + t:POST[p] + t + 1], in1=r2[:, :],
                                             op0=ALU.mult, op1=ALU.mult).then_inc(u_mul, 1)
                    dve.wait_ge(u_mul, k + 1)
                    dve.tensor_tensor(x[:, t, :], x[:, t, :], ut[:, t % 2, :], ALU.add).then_inc(x_new, 1)
                    if p < 4 and t:
                        low(p, t - 1)
                        add_squares(f"x{p}", t - 1, (t - 1) % 2, t == 1)
                if p < 4:
                    low(p, KD - 1)
                    add_squares(f"x{p}", KD - 1, (KD - 1) % 2, False)
                if p == 2:
                    for t in range(KD):
                        low_mix(p, t)

            dve.memset(ones[:, :], 1.0)
            dve.memset(eps[:, :], EPS).then_inc(memset_done, 1)
            for t in range(KD):
                dve.wait_ge(xT_done, t + 1)
                dve.tensor_copy(x[:, t, 0:SEQ], psum[:, 2 * (t % 2), :]).then_inc(xin_v, 1)
            split(0, 0, 0)
            split(1, 1, 1)
            for t in range(KD):
                low(0, t)
                add_squares("x0", t, t % 2, t == 0)

            def value_tile(i, u, first=False):
                j = 4 * i + u
                ahead(U_V, 4, i, u)
                dve.wait_ge(mm_done, U_V + j + 1)
                if first:
                    dve.wait_ge(r_ready, 1)
                wait(dve, z_done, j - 1)
                dve.tensor_tensor(halves(ut[:, u % 2, :]), acc(u % 2), halves(r1[:, :]), ALU.mult).then_inc(evac_sgu, 1)
                add_squares("v", j, u % 2, first)

            for u in range(4):
                value_tile(0, u, first=(u == 0))
            dve.wait_ge(gT_done, 1)
            dve.wait_ge(d_const, 16)
            for g in range(GROUPS):
                mm = dve.tensor_tensor(wmt[:, g, :], psum[:, 6 + g // 4, (g % 4) * P:(g % 4 + 1) * P], keep, ALU.mult)
            mm.then_inc(wm_ready, 1)
            with dve.Fori(1, 4) as i:
                for u in range(4):
                    value_tile(i, u)

            dve.wait_ge(z_done, KG)
            dve.tensor_copy(zs[:, :], zv[:, 0, :]).then_inc(zs_ready, 1)
            dve.wait_ge(d_bc, 32)

            def gate_tile(i, u, first=False, last=False):
                j, g = 4 * i + u, 2 * i + u // 2
                if not last:
                    dve.wait_ge(zT_done, j + 1)
                    dve.tensor_copy(zs[:, :], zv[:, bass.ds(j + 1, 1), :].rearrange("p o t -> p (o t)")).then_inc(zs_ready, 1)
                ahead(U_U, 4, i, u)
                if first:
                    dve.wait_ge(r_ready, GI["v"] + 1)
                dve.scalar_tensor_tensor(out=vsn[:, bass.ds(j, 1), :].rearrange("p o t -> p (o t)"),
                                         in0=zv[:, bass.ds(j, 1), SEQ:T].rearrange("p o t -> p (o t)"), scalar=pt[:, bass.ds(G_SGU + j, 1)],
                                         in1=r2[:, SEQ:T], op0=ALU.mult, op1=ALU.mult).then_inc(vs_ready, 1)
                dve.wait_ge(mm_done, U_U + j + 1)
                wait(dve, u_gelu, j)
                dve.tensor_tensor(halves(ut[:, 0, :]), acc(u % 2), halves(r1[:, :]), ALU.mult).then_inc(evac_sgu, 1)
                dve.wait_ge(vs_ready, j + 1)
                wait(dve, us_prod, j)
                dve.tensor_scalar(sT[:, SEQ:T], vsn[:, bass.ds(j, 1), :].rearrange("p o t -> p (o t)"), w00[:, bass.ds(g, 1)], bsb[:, bass.ds(g, 1), 0:1].rearrange("p o t -> p (o t)"),
                                  ALU.mult, ALU.add)
                dve.wait_ge(mix_done, j + 1)
                bias = bsb[:, bass.ds(g, 1), :].to_broadcast([P, 4, P])
                dve.scalar_tensor_tensor(out=sT[:, 0:SEQ].rearrange("p (c t) -> p c t", c=4), in0=psum[:, 5, :].rearrange("p (c t) -> p c t", c=4),
                                         scalar=pt[:, bass.ds(G_SGU + j, 1)], in1=bias, op0=ALU.mult, op1=ALU.add).then_inc(mix_read, 1)
                dve.wait_ge(mix_read, j + 1)
                dve.wait_ge(u_gelu, j + 1)
                wait(dve, usl_ready, j)
                dve.tensor_tensor(sq[:, 0, :], sT[:, :], ut[:, 1, :], ALU.mult).then_inc(us_prod, 1)
                dve.wait_ge(ush_ready, j + 1)
                dve.wait_ge(us_prod, j + 1)
                dve.tensor_tensor(usl[:, bass.ds(j, 1), :].rearrange("p o t -> p (o t)"), sq[:, 0, :],
                                  f32(ush[:, bass.ds(j, 1), :]).rearrange("p o t -> p (o t)"), ALU.subtract).then_inc(usl_ready, 1)

            gate_tile(0, 0, first=True)
            for u in range(1, 4):
                gate_tile(0, u)
            with dve.Fori(1, 3) as i:
                for u in range(4):
                    gate_tile(i, u)
            for u in range(4):
                gate_tile(3, u, last=(u == 3))
            for g in range(4):
                dve.wait_ge(vsT_done, g + 1)
                if g:
                    dve.wait_ge(cv_sent, 16 * g)
                dve.tensor_copy(cvo[0:NS, :, :].rearrange("p a b -> p (a b)"), psum[0:NS, 4 + g, :]).then_inc(cv_ready, 1)

            def wo(i, first=False):
                for e in range(2):
                    for half in range(2):
                        ahead(U_WO, 4, i, 2 * e + half)
                    add_squares("m_sgu", 2 * i + e, e, first and e == 0)
            wo(0, first=True)
            with dve.Fori(1, 4) as i:
                wo(i)
            update(1, m_raw)

            def mlp(l):
                def tile(i, u, first=False):
                    q, j = 4 * i + u, 2 * i + u // 2
                    f = (u % 2) * KF + j
                    Q, J, b = NF * l + q, KF * l + j, u % 2
                    ahead(U_UP[l], 4, i, u)
                    dve.wait_ge(mm_done, U_UP[l] + q + 1)
                    if first:
                        dve.wait_ge(r_ready, GI["x1" if l == 0 else "x3"] + 1)
                        dve.wait_ge(zpad, 1 + 2 * l)
                        if l == 0:
                            dve.wait_ge(cv_sent, 16 * 4)
                        else:
                            dve.wait_ge(n_sent, 16 * 10)
                    wait(dve, tails, Q - 1)
                    wait(dve, conv_done, Q - 1)
                    a_b = psum[:, 2 * b:2 * b + 2, :]
                    dve.tensor_tensor(ab[:, b, 2:2 + HB], a_b[:, 0, 0:HB], r1[:, 0:HB], ALU.mult)
                    dve.tensor_tensor(ab[:, b, 2 + HB:2 + SEQ], a_b[:, 1, 0:SEQ - HB], r1[:, HB:SEQ], ALU.mult)
                    dve.tensor_tensor(ab[:, b, 2 + SEQ:].rearrange("p (s k) -> p s k", k=3)[:, :, 2], a_b[:, 1, SEQ - HB:HB], r1[:, SEQ:T],
                                      ALU.mult).then_inc(evac_up, 1)
                    dve.wait_ge(evac_up, Q + 1)
                    dve.wait_ge(state_in, Q + 1)
                    wait(dve, prod_done, J)
                    w = [pt[:, bass.ds(conv_rows(l, k) + f, 1)] for k in range(3)]
                    bias = pt[:, bass.ds(C_CB + l * NF + f, 1)]
                    dve.tensor_scalar(cc[:, b, :], ab[:, b, 0:CW_], w[0], bias, ALU.mult, ALU.add).then_inc(conv_step, 1)
                    dve.wait_ge(conv_step, 2 * Q + 1)
                    dve.scalar_tensor_tensor(out=cc[:, b, :], in0=ab[:, b, 1:1 + CW_], scalar=w[1], in1=cc[:, b, :], op0=ALU.mult, op1=ALU.add)\
                       .then_inc(conv_step, 1)
                    dve.wait_ge(conv_step, 2 * Q + 2)
                    dve.scalar_tensor_tensor(out=cc[:, b, :], in0=ab[:, b, 2:2 + CW_], scalar=w[2], in1=cc[:, b, :], op0=ALU.mult, op1=ALU.add)\
                       .then_inc(conv_done, 1)
                    if b:
                        dve.wait_ge(gelu_done, J + 1)
                        dve.wait_ge(conv_done, Q + 1)
                        wait(dve, actl_ready, J)
                        dve.tensor_tensor(pr[:, 0:SEQ], cc[:, 0, 0:SEQ], cc[:, 1, 0:SEQ], ALU.mult)
                        smp = [cc[:, e, SEQ:].rearrange("p (s k) -> p s k", k=3)[:, :, 2] for e in range(2)]
                        dve.tensor_tensor(pr[:, SEQ:T], smp[0], smp[1], ALU.mult).then_inc(prod_done, 1)
                        dve.wait_ge(acth_ready, J + 1)
                        dve.wait_ge(prod_done, J + 1)
                        dve.tensor_tensor(actl[:, bass.ds(j, 1), :].rearrange("p o t -> p (o t)"), pr[:, :],
                                          f32(acth[:, bass.ds(j, 1), :]).rearrange("p o t -> p (o t)"), ALU.subtract).then_inc(actl_ready, 1)

                for u in range(4):
                    tile(0, u, first=(u == 0))
                with dve.Fori(1, NF // 4) as i:
                    for u in range(4):
                        tile(i, u)
                g = "m_ffn0" if l == 0 else "m_ffn1"

                def down(i, e, first=False, guard=False):
                    t = 2 * i + e
                    for w in range(4):
                        if guard:
                            ahead_static(U_DN[l] + 4 * t + w)
                        else:
                            ahead(U_DN[l], 8, i, 4 * e + w)
                    add_squares(g, t, e, first)

                down(0, 0, first=True)
                down(0, 1)
                with dve.Fori(1, 3) as i:
                    for e in range(2):
                        down(i, e)
                for e in range(2):
                    down(3, e, guard=True)

            mlp(0)
            update(2, m_raw)

            ahead_static(U_KV)
            dve.wait_ge(r_ready, GI["x2"] + 1)
            for t in range(KC):
                dve.wait_ge(mm_done, U_KV + t + 1)
                dve.tensor_tensor(halves(kvr[:, t, :]), acc(t), halves(r1[:, :]), ALU.mult).then_inc(evac_kv, 1)
            for t in range(KC):
                add_squares("kv", t, t % 2, t == 0)
            ahead_static(U_KV + 1)
            dve.wait_ge(mm_done, U_KV + 3)
            dve.tensor_tensor(halves(krr[:, :]), acc(0), halves(r1[:, :]), ALU.mult).then_inc(evac_kv, 1)
            ahead_static(U_KV + 2)
            ahead_static(U_DQ)
            dve.wait_ge(r_ready, GI["kv"] + 1)
            for t in range(KC):
                dve.scalar_tensor_tensor(out=ckt[:, t, :], in0=kvr[:, t, :], scalar=pt[:, G_KV + t:G_KV + t + 1], in1=r2[:, :],
                                         op0=ALU.mult, op1=ALU.mult).then_inc(ckt_ready, 1)
            for t in range(KQ):
                dve.wait_ge(mm_done, U_DQ + t + 1)
                dve.tensor_tensor(halves(cqr[:, t, :]), acc((3 + t) % 2), halves(r1[:, :]), ALU.mult).then_inc(evac_dq, 1)
                add_squares("cq", t, t % 2, t == 0)
                dve.wait_ge(cqh_ready, t + 1)
                dve.scalar_tensor_tensor(out=cql[:, t, :], in0=cqr[:, t, :], scalar=pt[:, G_Q + t:G_Q + t + 1], in1=f32(cqh[:, t, :]),
                                         op0=ALU.mult, op1=ALU.subtract).then_inc(cql_ready, 1)
                if t < KQ - 1:
                    ahead_static(U_DQ + t + 1)

            def rotate(dst, raw_, rot, tmp, done, step, n):
                dve.wait_ge(done, n + 1)
                dve.tensor_tensor(halves(tmp), rot, halves(sin), ALU.mult)
                dve.tensor_tensor(dst, raw_, cos, ALU.mult).then_inc(step, 1)
                dve.wait_ge(step, 2 * n + 1)
                dve.tensor_tensor(dst, dst, tmp, ALU.add).then_inc(step, 1)

            rotate(krt[:, :], krr[:, :], psum[:, 4:6, 0:HB], ut[:, 0, :], rotk_done, rotk_step, 0)
            dve.wait_ge(r_ready, GI["cq"] + 1)
            for t in range(12):
                if t % 2:
                    dve.wait_ge(mm_done, U_UQ + t // 2 + 1)
                else:
                    dve.wait_ge(uq_half, t // 2 + 1)
                dst = qn[:, t, :] if t < 8 else qrr[:, t - 8, :]
                dve.tensor_tensor(halves(dst), acc((7 + t) % 2), halves(r2[:, :]), ALU.mult).then_inc(evac_uq, 1)
                if t % 2:
                    ahead_static(U_UQ + t // 2)
            for t in range(4):
                dve.wait_ge(evac_uq, 12)
                wait(dve, rotq_step, 2 * t - 2)
                rotate(qr[:, t, :], qrr[:, t, :], acc((7 + t) % 2), ut[:, t % 2, :], rotq_done, rotq_step, t)

            dve.wait_ge(zpad, 2)
            dve.wait_ge(ql_done, 1)
            dve.wait_ge(qsel_done, 1)
            for c in range(KC):
                src = psum[:, 0, c * 64:(c + 1) * 64].rearrange("p (h s) -> p s h", h=H)
                dve.tensor_copy(qc[:, c, :].rearrange("p (s h) -> p s h", s=NS), src)
                dve.tensor_copy(qpad[:, c * 512:c * 512 + 576].rearrange("p (s x) -> p s x", x=72)[:, :, 0:H], src).then_inc(qpad_ready, 1)
            for e in range(2):
                src = psum[0:ROPE, 1, e * 32:(e + 1) * 32].rearrange("p (h s) -> p s h", h=4)
                dve.tensor_copy(qc[0:ROPE, 2, :].rearrange("p (s h e) -> p s h e", s=NS, e=2)[:, :, :, e], src)
                mm = dve.tensor_copy(qpad[0:ROPE, 1024:1024 + 576].rearrange("p (s x) -> p s x", x=72)[:, :, 0:H].rearrange(
                    "p s (h e) -> p s h e", e=2)[:, :, :, e], src)
            mm.then_inc(qpad_ready, 1)
            dve.wait_ge(sn_done, 1)
            dve.scalar_tensor_tensor(out=small[0:64, 24:32], in0=psum[0:64, 2, 0:NS], scalar=1.0, in1=own[0:64, :], op0=ALU.mult, op1=ALU.mult,
                                     accum_out=small[0:64, 1:2]).then_inc(sn_ready, 1)
            for g in range(0, 16, 2):
                dve.wait_ge(kv_done, g + 1)
                dst = kn[:, g, :] if g < 8 else v[:, (g - 8) // 2, 0:512]
                dve.tensor_copy(dst, psum[:, 4 + g % 4, :]).then_inc(kv_read_v, 1)

            for g in range(NS * NCH):
                dve.wait_ge(cT_done, g + 1)
                if g >= 2:
                    dve.wait_ge(sc_done, g - 1)
                dve.tensor_copy(kt[:, g % 2, 1, :], psum[:, 5, :]).then_inc(kt_v, 1)
            dve.wait_ge(sc_done, NS * NCH)
            dve.tensor_reduce(small[0:64, 0:1], psum[0:64, 0:4, :].rearrange("p a b -> p (a b)"), AX_X, ALU.max).then_inc(sm_v, 1)
            dve.wait_ge(sm_v, 1)
            dve.tensor_tensor(small[0:64, 0:1], small[0:64, 0:1], small[0:64, 1:2], ALU.max).then_inc(sm_v, 1)
            dve.wait_ge(sm_v, 2)
            dve.tensor_scalar(small[0:64, 2:3], small[0:64, 0:1], -SCALE, None, ALU.mult).then_inc(sm_v, 1)
            dve.wait_ge(sm_a, 2)
            dve.tensor_tensor(small[0:64, 5:6], small[0:64, 3:4], small[0:64, 4:5], ALU.add).then_inc(sm_v, 1)
            dve.wait_ge(sm_v, 4)
            dve.reciprocal(small[0:64, 6:7], small[0:64, 5:6]).then_inc(sm_v, 1)
            dve.wait_ge(sm_v, 5)
            dve.tensor_scalar(small[0:64, 16:24], own[0:64, :], small[0:64, 4:5], small[0:64, 6:7], ALU.mult, ALU.mult)
            dve.tensor_scalar(ps_sb[0:64, :], ps_sb[0:64, :], small[0:64, 6:7], None, ALU.mult).then_inc(sm_v, 1)
            dve.wait_ge(pnT_done, 1)
            dve.tensor_copy(pnd[0:NS, :], psum[0:NS, 6, 0:64]).then_inc(pnd_ready, 1)
            dve.wait_ge(olT_done, 1)
            for c in range(KC):
                mm = dve.tensor_copy(olT[:, c, :, :], psum[:, 4, c * 64:(c + 1) * 64].rearrange("p (s h) -> p h s", s=NS))
            mm.then_inc(olT_ready, 1)
            dve.wait_ge(os_done, 1)
            dve.tensor_copy(o[:, :, SEQ:T], psum[:, 5, 0:64].rearrange("p (h s) -> p h s", h=H)).then_inc(os_ready, 1)

            for g in range(4 * H + 5):
                if g < 4 * H:
                    b = g % 4
                    n = (b + 1) * P
                    dve.wait_ge(s_done, g + 1)
                    dve.tensor_tensor(psum[:, g % 4, b * P:n], psum[:, g % 4, b * P:n], cmask, ALU.add).then_inc(s_masked, 1)
                    dve.wait_ge(s_masked, g + 1)
                    dve.tensor_reduce(small[:, 12 + g % 2:13 + g % 2], psum[:, g % 4, 0:n], AX_X, ALU.max).then_inc(s_max, 1)
                    dve.wait_ge(s_max, g + 1)
                    if g >= 2:
                        dve.wait_ge(p_exp, g - 1)
                    dve.tensor_scalar(small[:, 8 + g % 2:9 + g % 2], small[:, 12 + g % 2:13 + g % 2], -SCALE, None, ALU.mult).then_inc(s_neg, 1)
                if 1 <= g <= 4 * H:
                    e, n = g - 1, ((g - 1) % 4 + 1) * P
                    dve.wait_ge(p_exp, e + 1)
                    dve.reciprocal(small[:, 14 + e % 2:15 + e % 2], small[:, 10 + e % 2:11 + e % 2]).then_inc(p_rec, 1)
                    dve.wait_ge(p_rec, e + 1)
                    dve.tensor_scalar(pp[:, e % 2, 0:n], pp[:, e % 2, 0:n], small[:, 14 + e % 2:15 + e % 2], None, ALU.mult).then_inc(p_norm, 1)
                if g >= 8 and g % 4 == 0:
                    h = g // 4 - 2
                    dve.wait_ge(ov_done, h + 1)
                    dve.tensor_copy(o[:, h, 0:SEQ], psum[:, 6 + h % 2, :]).then_inc(o_ready, 1)
            for h in range(H):
                dve.wait_ge(oh_ready, h + 1)
                dve.wait_ge(o_ready, h + 1)
                dve.tensor_tensor(xl[:, h, :], o[:, h, :], f32(xh[:, h, :]), ALU.subtract).then_inc(ol_ready, 1)
            for t in range(KD):
                ahead_static(U_O + t)
                add_squares("m_attn", t, t % 2, t == 0)
            update(3, m_attn)
            mlp(1)
            update(4, m_raw)
            for c in range(5):
                rows = P if c < 4 else NS
                dve.wait_ge(yT_done, c + 1)
                dve.tensor_copy(yn[0:rows, c, 0:512], psum[0:rows, 2 * (c % 2), :]).then_inc(y_ready_v, 1)


_INS = ["x_prompt", "x_sample", "cache_ckv", "cache_kr", "state_conv", "page_table", "pre_mix_g", "post_mix_g", "pre_ffn_g",
        "post_ffn_g", "w_in_a", "sgu_g", "w_s", "b_s", "w_out_a", "kv_in_g", "w_dkv", "kv_g", "w_uk", "w_uv", "w_dq", "q_g",
        "w_uq", "w_o", "w_up", "conv_w", "conv_b", "w_down"]
_OUTS = [("y_prompt", (1, SEQ, D)), ("y_sample", (NS, 1, D)), ("new_ckv_prompt", (1, SEQ, CL)), ("new_kr_prompt", (1, SEQ, ROPE)),
         ("new_conv_prompt", (DEPTH, 1, 2, 2 * DFF)), ("new_ckv_sample", (NS, 1, CL)), ("new_kr_sample", (NS, 1, ROPE)),
         ("new_conv_sample", (DEPTH, NS, 2, 2 * DFF)), ("new_chunkv_sample", (1, NS, 1, GW))]


def kernel(**inputs):
    import concourse.bacc as bacc
    from concourse.bass_utils import run_bass_kernel_spmd

    nc = bacc.Bacc("TRN2", target_bir_lowering=False, num_devices=1)
    arrays, a, outs = {}, {}, {}
    for name in _INS + ["consts"]:
        v = constants() if name == "consts" else np.ascontiguousarray(inputs[name])
        arrays[f"in_{name}"] = v
        a[name] = nc.dram_tensor(f"in_{name}", v.shape, mybir.dt.from_np(v.dtype), kind="ExternalInput").ap()
    for name, shape in _OUTS:
        outs[name] = nc.dram_tensor(f"out_{name}", shape, F32, kind="ExternalOutput").ap()
    trunk(nc, a, outs)
    r = run_bass_kernel_spmd(nc, [arrays], core_ids=[0])
    return tuple(r.results[0][f"out_{name}"] for name, _ in _OUTS)
```

```python
from contextlib import ExitStack

import numpy as np

import concourse.bass as bass
from concourse import mybir

ALU = mybir.AluOpType
ACT = mybir.ActivationFunctionType
F32 = mybir.dt.float32
F32R = mybir.dt.float32r
I32 = mybir.dt.int32
AX_X = mybir.AxisListType.X

P = 128
D = 1024
KD = D // P
SEQ, NS = 512, 8
T = SEQ + NS
HB = T // 2
DEPTH = 2
EPS = 1e-6
GW = 2048
KG = GW // P
GROUPS = 8
DFF = 2816
KF = DFF // P
NF = 2 * KF
H, NOPE, ROPE = 8, 128, 64
QL, CL = 512, 256
KQ, KC = QL // P, CL // P
PAST, PAGE = 2048, 128
NPG = PAST // PAGE
SCALE = float(NOPE + ROPE) ** -0.5
CH = 4
NCH = NPG // CH
NG = NS * NCH
RING = 2 * NCH
CN_SLOTS = 3
PW = 32 + H

U_V, U_U, U_WO = 0, 16, 32
U_UP, U_DN = [48, 145], [92, 189]
U_KV, U_DQ, U_UQ, U_O = 124, 127, 131, 137
U_END = 221
STAGES = 4
DN_SPLIT = [(0, 6), (6, 6), (12, 5), (17, 5)]

G_PREMIX, G_POSTMIX, G_PREFFN, G_POSTFFN = 0, 16, 32, 48
G_SGU, G_KVIN, G_KV, G_Q = 64, 80, 88, 90
C_CB, C_CW = 94, 182
C_ST = C_CW + DEPTH * 3 * NF
C_END = C_ST + DEPTH * NS * 2 * NF
NBLK = (C_END + P - 1) // P

GROUPS_SQ = [("x0", KD, D), ("v", KG, GW), ("m_sgu", KD, D), ("x1", KD, D), ("m_ffn0", KD, D), ("x2", KD, D),
             ("kv", KC, CL), ("cq", KQ, QL), ("m_attn", KD, D), ("x3", KD, D), ("m_ffn1", KD, D)]
GI = {n: i for i, (n, _, _) in enumerate(GROUPS_SQ)}
SQB = {n: sum(c for _, c, _ in GROUPS_SQ[:i]) for i, (n, _, _) in enumerate(GROUPS_SQ)}

CONST_COLS = 4 * P + 2 * T + NS

ROWS = [("pre_mix_g", 16), ("post_mix_g", 16), ("pre_ffn_g", 16), ("post_ffn_g", 16), ("sgu_g", 16), ("kv_in_g", 8),
        ("kv_g", 2), ("q_g", 4), ("conv_b", DEPTH * NF), ("conv_w", DEPTH * 3 * NF), ("state_conv", DEPTH * NS * 2 * NF)]


def pack_pieces():
    pieces, col = [], 0
    for name, rows in ROWS:
        r = 0
        while r < rows:
            n = min(rows - r, P - col % P)
            pieces.append((name, r, col // P, col % P, n))
            r, col = r + n, col + n
    assert col == C_END
    return pieces


def rows_of(ap):
    names = "abcdef"[:len(ap.shape) - 1]
    return ap.rearrange(f"{' '.join(names)} (k z) -> ({' '.join(names)} k) z", z=P)


PACK = pack_pieces()
PACK0 = 16 * sum(p[2] < 4 for p in PACK)
PACK1 = 16 * sum(p[2] >= 4 for p in PACK)


def constants():
    c = np.zeros((P, CONST_COLS), np.float32)
    c[:, 0:P] = np.eye(P, dtype=np.float32)
    half = ROPE // 2
    for m in range(P):
        d = m % ROPE
        c[m + half if d < half else m - half, P + m] = -1.0 if d < half else 1.0
    c[:, 2 * P:3 * P] = np.where(np.arange(P)[None, :] <= np.arange(P)[:, None], 0.0, -1e30)
    inv = np.float32(1.0) / (np.float32(10000.0) ** (np.arange(half, dtype=np.float32) / np.float32(half)))
    pos = np.concatenate([np.arange(SEQ), np.full(NS, PAST)]).astype(np.float32)
    ang = (pos[None, :] * inv[:, None]).astype(np.float32)
    c[:, 3 * P:3 * P + T] = np.tile(np.cos(ang), (4, 1))
    c[:, 3 * P + T:3 * P + 2 * T] = np.tile(np.sin(ang), (4, 1))
    for r in range(NS * H):
        c[r, 3 * P + 2 * T + r // H] = 1.0
    c[:, 3 * P + 2 * T + NS:] = np.arange(P)[:, None] <= np.arange(P)[None, :]
    return c


def dmas_of_unit(n):
    if n == U_KV + 2:
        return 2
    if U_UQ <= n < U_UQ + 4:
        return 2
    if U_UQ + 4 <= n < U_UQ + 6:
        return 4
    return 1


def staged(n):
    return 16 * sum(dmas_of_unit(m) for m in range(n % STAGES, n + 1, STAGES))


def trunk(nc, a, outs):
    ctx = ExitStack()
    with ctx:
        top = [(nc.sbuf_base + 31) // 32 * 32]

        def at(name, shape, offset, dt=F32):
            return nc.alloc_sbuf_tensor_at(name, [P] + shape, dt, offset=offset)

        def size(shape):
            return (4 * int(np.prod(shape)) + 31) // 32 * 32

        def sb(name, shape, dt=F32):
            off = top[0]
            top[0] += size(shape)
            return at(name, shape, off, dt)

        def plan(base, *items):
            out = []
            for name, shape, dt in items:
                out.append(at(name, shape, base, dt))
                base += size(shape)
            assert base <= nc.sbuf_usable_end, (name, base)
            return out + [base]

        x = sb("x", [KD, T])
        xg_base = top[0]
        xh, xl = sb("xh", [KD, T], F32R), sb("xl", [KD, T], F32R)
        ws_base = top[0]
        ws = sb("ws", [STAGES, 1024])
        wh, wl = sb("wh", [2, 1024], F32R), sb("wl", [2, 1024], F32R)
        pt = sb("pt", [C_END])
        cst = sb("cst", [CONST_COLS])
        ones = sb("ones", [P])
        eps = sb("eps", [1])
        r1, r2 = sb("r1", [T]), sb("r2", [T])
        tmp_base = top[0]
        sq, sqa, ut = sb("sq", [2, T]), sb("sqa", [T]), sb("ut", [2, T])
        arena = top[0]
        ident, perm = cst[:, 0:P], cst[:, P:2 * P]
        cmask = cst[:, 2 * P:3 * P]
        cos, sin = cst[:, 3 * P:3 * P + T], cst[:, 3 * P + T:3 * P + 2 * T]
        own = cst[:, 3 * P + 2 * T:3 * P + 2 * T + NS]
        keep = cst[:, 3 * P + 2 * T + NS:]
        m_raw = at("m_raw", [KD, T], xg_base)

        zv, usl, wmt, bsb, vsn, w00, rn, sT, vn, zs, cvo, wn, pn, gu_end = plan(
            arena, ("zv", [KG, T], F32), ("usl", [KG, T], F32R), ("wmt", [GROUPS, P], F32), ("bsb", [GROUPS, P], F32),
            ("vsn", [KG, NS], F32), ("w00", [GROUPS], F32), ("rn", [CH + 1], F32),
            ("sT", [T], F32), ("vn", [CH, P], F32), ("zs", [T], F32), ("cvo", [CH, P], F32),
            ("wn", [GROUPS, P], F32), ("pn", [NBLK, P], F32))
        ush = at("ush", [KG, T], arena, F32R)
        xn, xs, _ = plan(arena, ("xn", [4, D], F32), ("xs", [D], F32))
        acth, actl, ab, cc, _ = plan(
            arena, ("acth", [KF, T], F32R), ("actl", [KF, T], F32R), ("ab", [2, 2 + SEQ + 3 * NS], F32),
            ("cc", [2, SEQ + 3 * NS], F32))
        cs = at("cs", [2 + NS, NF], tmp_base - size([T]))
        pr, _ = plan(tmp_base + 3 * size([T]), ("pr", [T], F32))
        csn, _ = plan(tmp_base + 3 * size([T]), ("csn", [5, P], F32))
        CW_ = SEQ + 3 * NS
        xkh, xkl, cqh, cql, kvr, krr, cqr, proj_end = plan(
            arena, ("xkh", [KD, T], F32R), ("xkl", [KD, T], F32R), ("cqh", [KQ, T], F32R), ("cql", [KQ, T], F32R),
            ("kvr", [KC, T], F32), ("krr", [T], F32), ("cqr", [KQ, T], F32))
        ukt = at("ukt", [H, CL], arena)
        lat_h, lat_l, ckb, ckt, krt, uv, uk, qc, qh, ql, smp, pgt, cksn, small, _ = plan(
            arena, ("lat_h", [RING, CH, CL], F32R), ("lat_l", [RING, CH, CL], F32R), ("ckb", [NS, CL], F32), ("ckt", [KC, T], F32),
            ("krt", [T], F32), ("uv", [KC, D], F32), ("uk", [KC, D], F32), ("qc", [3, NS * H], F32), ("qh", [3, NS * H], F32R),
            ("ql", [3, NS * H], F32R), ("smp", [13 * NS], F32), ("pgt", [P], I32), ("cksn", [320], F32),
            ("small", [16], F32))
        ident_r, olT, pick, fold, fold_r, dg, r2_end = plan(
            tmp_base - size([T]), ("ident_r", [P], F32R), ("olT", [KC, H, NS], F32), ("pick", [NS, H], F32), ("fold", [H], F32),
            ("fold_r", [H], F32), ("dg", [H], F32))
        assert r2_end <= tmp_base
        assert proj_end <= arena + 2 * size([RING, CH, CL])
        cn, kt0, kr2, pts, cn_end = plan(
            ws_base, ("cn", [CN_SLOTS, CH, 320], F32), ("kt0", [5, 512], F32R), ("kr2", [2, CH, P], F32R), ("pts", [NPG, PW], F32R))
        assert cn_end <= ws_base + 2 * size([STAGES, 1024])
        kt1 = at("kt1", [5, 512], tmp_base, F32R)
        assert size([5, 512]) <= arena - tmp_base
        kt = [kt0, kt1]
        osn = at("osn", [CL], tmp_base - 2 * size([T]))
        qn, qrr, qr, _ = plan(xg_base, ("qn", [H, T], F32), ("qrr", [4, T], F32), ("qr", [4, T], F32))
        ps_sb = at("ps_sb", [PAST], xg_base + size([H, T]))
        kn, v, o, pp, ppt, okn, pr_end = plan(
            arena, ("kn", [H, SEQ], F32), ("v", [4, D], F32), ("o", [H, T], F32), ("pp", [2, SEQ], F32), ("ppt", [2, 4, SEQ], F32),
            ("okn", [2, 320], F32))
        assert pr_end <= arena + 2 * size([RING, CH, CL]) + size([NS, CL])
        m_attn = at("m_attn", [KD, T], arena)
        yn, _ = plan(arena, ("yn", [5, D], F32))

        psum = ctx.enter_context(nc.psum_tensor("psum", [P, 8, 512], F32))

        def S(name):
            return ctx.enter_context(nc.semaphore(name))

        d_stage = [S(f"d_stage{i}") for i in range(STAGES)]
        d_const, d_pack0, d_pack1, d_xs = S("d_const"), S("d_pack0"), S("d_pack1"), S("d_xs")
        d_x = [S(f"d_x{i}") for i in range(4)]
        d_gate, d_bc, d_out, d_state, cv_sent = (S(n) for n in ("d_gate", "d_bc", "d_out", "d_state", "cv_sent"))
        d_uk, d_pages = S("d_uk"), S("d_pages")
        d_cn = [S(f"d_cn{i}") for i in range(CN_SLOTS)]
        w_high, w_low, mm_done = S("w_high"), S("w_low"), S("mm_done")
        sq_done, sq_added, ss_done, ln_done, r_ready = S("sq_done"), S("sq_added"), S("ss_done"), S("ln_done"), S("r_ready")
        x_new, u_mul, xh_ready, xl_ready, xkh_ready, xkl_ready = (S(n) for n in (
            "x_new", "u_mul", "xh_ready", "xl_ready", "xkh_ready", "xkl_ready"))
        xT_done, xin_v, xin_s = S("xT_done"), S("xin_v"), S("xin_s")
        memset_done, packT_done, pack_ready = S("memset_done"), S("packT_done"), S("pack_ready")
        gT_done, wm_ready = S("gT_done"), S("wm_ready")
        evac_sgu, z_done, u_gelu, zs_ready, zT_done, vn_ready = (S(n) for n in (
            "evac_sgu", "z_done", "u_gelu", "zs_ready", "zT_done", "vn_ready"))
        rT_done, rn_ready, mix_done, mix_read, vs_ready, us_prod, ush_ready, usl_ready = (S(n) for n in (
            "rT_done", "rn_ready", "mix_done", "mix_read", "vs_ready", "us_prod", "ush_ready", "usl_ready"))
        vsT_done, cv_ready = S("vsT_done"), S("cv_ready")
        evac_up, state_in, tails, conv_step, conv_done, gelu_done, prod_done, acth_ready, actl_ready = (S(n) for n in (
            "evac_up", "state_in", "tails", "conv_step", "conv_done", "gelu_done", "prod_done", "acth_ready", "actl_ready"))
        csT_done, csn_ready, csn_sent, m_ready = S("csT_done"), S("csn_ready"), S("csn_sent"), S("m_ready")
        evac_kv, evac_dq, evac_uq, rotk_done, rotk_step, ck_step, ckt_ready = (S(n) for n in (
            "evac_kv", "evac_dq", "evac_uq", "rotk_done", "rotk_step", "ck_step", "ckt_ready"))
        cqh_ready, cql_ready, rotq_done, rotq_step = (S(n) for n in (
            "cqh_ready", "cql_ready", "rotq_done", "rotq_step"))
        ukT_done, ukt_ready, ql_done, qc_ready, qh_ready, ql_ready, qsel_done, sn_done, sn_ready, zpad = (S(n) for n in (
            "ukT_done", "ukt_ready", "ql_done", "qc_ready", "qh_ready", "ql_ready", "qsel_done", "sn_done", "sn_ready", "zpad"))
        pick_ready, ckb_done, ckb_ready, fold_ready = S("pick_ready"), S("ckb_done"), S("ckb_ready"), S("fold_ready")
        kv_done, kv_read_a, kv_read_v, nT_done, n_ready, n_sent = (S(n) for n in (
            "kv_done", "kv_read_a", "kv_read_v", "nT_done", "n_ready", "n_sent"))
        c_high, c_low, cT_done, kt_a, kt_v, sc_done = (S(n) for n in ("c_high", "c_low", "cT_done", "kt_a", "kt_v", "sc_done"))
        mx_done, mx_all, neg_ready, e_done, own_ready, tot_ready, rec_ready, foldr_ready, dg_ready = (S(n) for n in (
            "mx_done", "mx_all", "neg_ready", "e_done", "own_ready", "tot_ready", "rec_ready", "foldr_ready", "dg_ready"))
        idr_ready = S("idr_ready")
        okn_sent = [S(f"okn_sent{i}") for i in range(2)]
        pT_done, pts_h, pts_l, pv_done, osn_ready, olp_done, olT_ready, os_done, os_ready = (S(n) for n in (
            "pT_done", "pts_h", "pts_l", "pv_done", "osn_ready", "olp_done", "olT_ready", "os_done", "os_ready"))
        s_done, s_masked, s_max, s_neg, p_exp, p_rec, p_norm, ppT_done, ppt_ready, ov_done, o_ready = (S(n) for n in (
            "s_done", "s_masked", "s_max", "s_neg", "p_exp", "p_rec", "p_norm", "ppT_done", "ppt_ready", "ov_done", "o_ready"))
        oh_ready, ol_ready, uq_half = S("oh_ready"), S("ol_ready"), S("uq_half")
        yT_done, y_ready_v, y_ready_a = S("yT_done"), S("y_ready_v"), S("y_ready_a")

        def wait(eng, sem, value):
            if not isinstance(value, int) or value > 0:
                eng.wait_ge(sem, value)

        def f32(ap):
            return ap.bitcast(F32)

        def halves(ap):
            return ap.rearrange("p (h t) -> p h t", h=2)

        def acc(slot):
            return psum[:, 2 * slot:2 * slot + 2, 0:HB]

        def conv_rows(l, k):
            return C_CW + (l * 3 + k) * NF

        POST = [None, G_POSTMIX, G_POSTFFN, G_POSTMIX + KD, G_POSTFFN + KD]
        PRE = [G_PREMIX, G_PREFFN, G_PREMIX + KD, G_PREFFN + KD, None]

        def add_squares(eng, name, t, slot):
            n = SQB[name] + t
            if isinstance(t, int) and t == 0:
                return
            eng.wait_ge(sq_done, n + 1)
            if isinstance(t, int) and t == 1:
                wait(eng, sq_added, SQB[name])
                wait(eng, ss_done, GI[name])
                eng.tensor_tensor(sqa[:, :], sq[:, 0, :], sq[:, 1, :], ALU.add).then_inc(sq_added, 2)
            else:
                eng.wait_ge(sq_added, n)
                eng.tensor_tensor(sqa[:, :], sqa[:, :], sq[:, slot, :], ALU.add).then_inc(sq_added, 1)

        block = ctx.enter_context(nc.Block())

        @block.sync
        def _(sp):
            def free(n):
                wait(sp, w_low, n - (STAGES - 1))

            def put(n, slot, src, k, cols=P, off=0):
                dst = ws[:, slot, off:off + k * cols].rearrange("p (k c) -> p k c", c=cols)
                sp.dma_start(dst, src.rearrange("(k p) c -> p k c", p=P)).then_inc(d_stage[slot], 16)

            sp.dma_start(cst[:, :], a["consts"]).then_inc(d_const, 16)
            for c in range(4):
                sp.dma_start(xn[:, c, :], a["x_prompt"][0, c * P:(c + 1) * P, :]).then_inc(d_x[c], 16)
            sp.dma_start(xs[0:NS, :], a["x_sample"][:, 0, :]).then_inc(d_xs, 16)

            w_in, w_out = a["w_in_a"][0], a["w_out_a"][0]
            for phase, base, col in ((0, U_V, GW), (1, U_U, 0)):
                def v_units(i, base=base, col=col):
                    for u in range(4):
                        n = base + 4 * i + u
                        free(n)
                        put(n, u, w_in[:, bass.ds(col + (4 * i + u) * P, P)], KD)
                if phase == 0:
                    v_units(0)
                with sp.Fori(1 if phase == 0 else 0, 4) as i:
                    v_units(i)
            with sp.Fori(0, 4) as i:
                for u in range(4):
                    n = U_WO + 4 * i + u
                    free(n)
                    put(n, u, w_out[(u % 2) * D:(u % 2 + 1) * D, bass.ds((2 * i + u // 2) * P, P)], KD)

            def mlp(l):
                up, down = a["w_up"][l], a["w_down"][l]
                with sp.Fori(0, NF // 4) as i:
                    for u in range(4):
                        n = U_UP[l] + 4 * i + u
                        free(n)
                        put(n, (U_UP[l] + u) % STAGES, up[:, bass.ds((u % 2) * DFF + (2 * i + u // 2) * P, P)], KD)
                with sp.Fori(0, KD) as i:
                    for u, (k0, k) in enumerate(DN_SPLIT):
                        n = U_DN[l] + 4 * i + u
                        free(n)
                        put(n, (U_DN[l] + u) % STAGES, down[k0 * P:(k0 + k) * P, bass.ds(i * P, P)], k)

            mlp(0)
            w_dkv, w_dq, w_uq, w_o = a["w_dkv"], a["w_dq"][0], a["w_uq"][0], a["w_o"][0]
            for t in range(3):
                n = U_KV + t
                free(n)
                if t < 2:
                    put(n, n % STAGES, w_dkv[:, t * P:(t + 1) * P], KD)
                else:
                    for c in range(2):
                        dst = ws[:, n % STAGES, :].rearrange("p (k c) -> p k c", c=P)[:, :, c * ROPE:(c + 1) * ROPE]
                        sp.dma_start(dst, w_dkv[:, CL:CL + ROPE].rearrange("(k p) c -> p k c", p=P)).then_inc(
                            d_stage[n % STAGES], 16)
            for t in range(KQ):
                n = U_DQ + t
                free(n)
                put(n, n % STAGES, w_dq[:, t * P:(t + 1) * P], KD)
            for j in range(6):
                n = U_UQ + j
                free(n)
                for e in range(2):
                    if j < 4:
                        put(n, n % STAGES, w_uq[:, (2 * j + e) * (NOPE + ROPE):(2 * j + e) * (NOPE + ROPE) + NOPE], KQ, off=e * KQ * P)
                    else:
                        for hh in range(2):
                            col = (4 * (j - 4) + 2 * e + hh) * (NOPE + ROPE) + NOPE
                            dst = ws[:, n % STAGES, e * KQ * P:(e + 1) * KQ * P].rearrange("p (k c) -> p k c", c=P)
                            sp.dma_start(dst[:, :, hh * ROPE:(hh + 1) * ROPE],
                                         w_uq[:, col:col + ROPE].rearrange("(k p) c -> p k c", p=P)).then_inc(
                                d_stage[n % STAGES], 16)
            sp.wait_ge(d_pages, 16)
            for g in range(NG):
                if g < CN_SLOTS:
                    sp.wait_ge(w_low, U_O)
                else:
                    sp.wait_ge(c_low, g - CN_SLOTS + 1)
                for j in range(CH):
                    page = sp.value_load(pgt[0:1, g * CH + j:g * CH + j + 1], min_val=0, max_val=a["cache_ckv"].shape[0] - 1)
                    sp.dma_start(cn[:, g % CN_SLOTS, j, 0:CL], a["cache_ckv"][bass.ds(page, 1), :, :].rearrange(
                        "o p c -> (o p) c")).then_inc(d_cn[g % CN_SLOTS], 16)
                    sp.dma_start(cn[:, g % CN_SLOTS, j, CL:CL + ROPE], a["cache_kr"][bass.ds(page, 1), :, :].rearrange(
                        "o p c -> (o p) c")).then_inc(d_cn[g % CN_SLOTS], 16)
            sp.wait_ge(c_low, NG)
            sp.wait_ge(sc_done, NG)
            for t in range(KD):
                n = U_O + t
                free(n)
                put(n, n % STAGES, w_o[:, t * P:(t + 1) * P], KD)
            mlp(1)

            for c in range(5):
                sp.wait_ge(y_ready_v, c + 1)
                sp.wait_ge(y_ready_a, c + 1)
                if c < 4:
                    sp.dma_start(outs["y_prompt"][0, c * P:(c + 1) * P, :], yn[:, c, :]).then_inc(d_out, 16)
                else:
                    sp.dma_start(outs["y_sample"][:, 0, :], yn[0:NS, c, :]).then_inc(d_out, 16)
            sp.wait_ge(d_out, 16 * 5)

        @block.gpsimd
        def _(pool):
            pool.dma_start(outs["new_conv_sample"][:, :, 0, :], a["state_conv"][:, :, 1, :]).then_inc(d_state, 16)

            def mlp(l):
                def tile(i, u):
                    q = NF * l + 4 * i + u
                    f = (u % 2) * KF + 2 * i + u // 2
                    wait(pool, conv_done, q - 1)
                    st = pt[:, C_ST + l * NS * 2 * NF:C_ST + (l + 1) * NS * 2 * NF].rearrange(
                        "p (s k f) -> p s k f", s=NS, k=2)
                    dst = ab[:, u % 2, 2 + SEQ:].rearrange("p (s k) -> p s k", k=3)
                    pool.tensor_copy(dst[:, :, 0:2], st[:, :, :, bass.ds(f, 1)].rearrange("p s k o -> p s (k o)")).then_inc(state_in, 1)
                    pool.wait_ge(evac_up, q + 1)
                    pool.tensor_copy(cs[:, 0:2, bass.ds(f, 1)].rearrange("p k o -> p (k o)"), ab[:, u % 2, SEQ:SEQ + 2])
                    pool.tensor_copy(cs[:, 2:2 + NS, bass.ds(f, 1)].rearrange("p k o -> p (k o)"), dst[:, :, 2]).then_inc(tails, 1)

                if l == 0:
                    pool.wait_ge(pack_ready, 4)
                    pool.wait_ge(usl_ready, KG)
                else:
                    pool.wait_ge(csT_done, 1)
                    pool.wait_ge(ol_ready, H)
                for t in range(KD):
                    add_squares(pool, f"x{1 + 2 * l}", t, t % 2)
                pool.wait_ge(x_new, KD * (1 + 2 * l))
                pool.memset(ab[:, :, 0:2], 0.0).then_inc(zpad, 1)
                for u in range(4):
                    tile(0, u)
                with pool.Fori(1, NF // 4) as i:
                    for u in range(4):
                        tile(i, u)
                pool.wait_ge(csn_ready, l + 1)
                pool.dma_start(outs["new_conv_prompt"][l, 0].rearrange("k (f c) -> (k f) c", c=P),
                               csn[0:2 * NF, 0, :]).then_inc(csn_sent, 16)
                for g in range(4):
                    for e in range(2):
                        pool.dma_start(outs["new_conv_sample"][l, 2 * g + e, 1].rearrange("(f c) -> f c", c=P),
                                       csn[e * NF:(e + 1) * NF, g + 1, :]).then_inc(csn_sent, 16)

            for g in range(4):
                pool.wait_ge(cv_ready, g + 1)
                pool.dma_start(outs["new_chunkv_sample"][0, :, 0, g * 512:(g + 1) * 512],
                               cvo[0:NS, :, :].rearrange("p a b -> p (a b)")).then_inc(cv_sent, 16)
            mlp(0)
            for t in range(KD):
                add_squares(pool, "x2", t, t % 2)
            pool.wait_ge(mm_done, U_DN[0] + 4 * KD)
            pool.dma_start(uk[:, :, :], a["w_uk"].rearrange("(k p) h d -> p k (h d)", p=P)).then_inc(d_uk, 16)
            pool.dma_start(uv[:, :, :], a["w_uv"].rearrange("(k p) h d -> p k (h d)", p=P)).then_inc(d_uk, 16)
            pool.dma_start(pgt[0:1, :], a["page_table"].rearrange("(o s) g -> o (s g)", o=1)).then_inc(d_pages, 16)
            for c in range(5):
                pool.wait_ge(n_ready, c + 1)
                r0 = (c - 1) * P
                src = okn[:, (c - 1) % 2, :] if c else cksn[0:NS, :]
                dst_c = outs["new_ckv_prompt"][0, r0:r0 + P, :] if c else outs["new_ckv_sample"][:, 0, :]
                dst_r = outs["new_kr_prompt"][0, r0:r0 + P, :] if c else outs["new_kr_sample"][:, 0, :]
                sent = okn_sent[(c - 1) % 2] if c else n_sent
                pool.dma_start(dst_c, src[:, 0:CL]).then_inc(sent, 16)
                pool.dma_start(dst_r, src[:, CL:CL + ROPE]).then_inc(sent, 16)
            mlp(1)
            pool.wait_ge(d_state, 16)
            pool.wait_ge(cv_sent, 16 * 4)
            pool.wait_ge(n_sent, 32)
            for sent in okn_sent:
                pool.wait_ge(sent, 64)
            pool.wait_ge(csn_sent, 16 * 9 * DEPTH)

        @block.tensor
        def _(pe):
            def product(n, slot, nslot, k, kk, rh, rl, first, last):
                hw, lw = wh[:, nslot, kk * P:(kk + 1) * P], wl[:, nslot, kk * P:(kk + 1) * P]
                for w, r, st, en in ((hw, rh, first, False), (hw, rl, False, False), (lw, rh, False, last)):
                    for b in range(2):
                        mm = pe.matmul(psum[:, 2 * slot + b, 0:HB], w, r[:, k, b * HB:(b + 1) * HB], start=st, stop=en)
                return mm

            def unit(n, nslot, slot, ks, rh, rl, first, last, ready=None, koff=0):
                pe.wait_ge(w_low, n + 1)
                for kk, k in enumerate(ks):
                    if ready is not None:
                        for sem, v in ready:
                            pe.wait_ge(sem, v + k + 1)
                    mm = product(n, slot, nslot, k, koff + kk, rh, rl, first and kk == 0, last and kk == len(ks) - 1)
                mm.then_inc(mm_done, 1)

            def two_units(n, rh, rl, ready):
                pe.wait_ge(w_low, n + 2)
                for k in range(KD):
                    for sem, v in ready:
                        pe.wait_ge(sem, v + k + 1)
                    for e in range(2):
                        mm = product(n + e, e, (n + e) % 2, k, k, rh, rl, k == 0, k == KD - 1)
                        if k == KD - 1:
                            mm.then_inc(mm_done, 1)

            def rms(name):
                g = GI[name]
                pe.wait_ge(sq_added, SQB[name] + GROUPS_SQ[g][1])
                wait(pe, ln_done, g)
                for b in range(2):
                    mm = pe.matmul(psum[:, 6 + b, 0:HB], ones[:, :], sqa[:, b * HB:(b + 1) * HB], start=True, stop=True)
                mm.then_inc(ss_done, 1)

            pe.wait_ge(d_const, 16)
            pe.wait_ge(memset_done, 1)

            def pack(g):
                for b in range(4 * g, min(4 * g + 4, NBLK)):
                    rows = min(P, C_END - b * P)
                    mm = pe.transpose(psum[:, 4 + g % 2, (b % 4) * P:(b % 4) * P + rows], pn[0:rows, b, :], ident[0:rows, 0:rows])
                mm.then_inc(packT_done, 1)

            pe.wait_ge(d_xs, 16)
            for t in range(KD):
                if t >= 2:
                    pe.wait_ge(xin_v, t - 1)
                    pe.wait_ge(xin_s, t - 1)
                for c in range(4):
                    if t == 0:
                        pe.wait_ge(d_x[c], 16)
                    pe.transpose(psum[:, 2 * (t % 2), c * P:(c + 1) * P], xn[:, c, t * P:(t + 1) * P], ident)
                pe.transpose(psum[:, 2 * (t % 2) + 1, 0:NS], xs[0:NS, t * P:(t + 1) * P], ident[0:NS, 0:NS]).then_inc(xT_done, 1)
                if t == 0:
                    pe.wait_ge(d_pack0, PACK0)
                    pack(0)

            pe.wait_ge(xin_v, KD)
            pe.wait_ge(xin_s, KD)
            two_units(U_V, xh, xl, [(xl_ready, 0)])
            rms("x0")
            for t in range(2, 4):
                pe.wait_ge(evac_sgu, t - 1)
                unit(U_V + t, t % 2, t % 2, range(KD), xh, xl, True, True)
            pe.wait_ge(d_pack1, PACK1)
            for g in range(1, 4):
                wait(pe, pack_ready, g - 1)
                pack(g)
            pe.wait_ge(d_gate, 16)
            pe.wait_ge(ln_done, 1)
            for g in range(GROUPS):
                mm = pe.transpose(psum[:, 6 + g // 4, (g % 4) * P:(g % 4 + 1) * P], wn[:, g, :], ident)
            mm.then_inc(gT_done, 1)
            with pe.Fori(1, 4) as i:
                for u in range(4):
                    t = 4 * i + u
                    pe.wait_ge(evac_sgu, t - 1)
                    unit(U_V + t, u % 2, u % 2, range(KD), xh, xl, True, True)

            def turn_values():
                for c in range(4):
                    mm = pe.transpose(psum[:, 4, c * P:(c + 1) * P], zs[:, c * P:(c + 1) * P], ident)
                mm.then_inc(zT_done, 1)

            def gate_tile(i, u, first=False):
                j = 4 * i + u
                pe.wait_ge(zs_ready, j + 1)
                wait(pe, vn_ready, j)
                if first:
                    pe.wait_ge(pack_ready, 4)
                    pe.wait_ge(wm_ready, 1)
                turn_values()
                pe.wait_ge(evac_sgu, U_U + j - 1)
                unit(U_U + j, u % 2, u % 2, range(KD), xh, xl, True, True)
                if first:
                    rms("v")
                    pe.wait_ge(r_ready, GI["v"] + 1)
                    for c in range(4):
                        mm = pe.transpose(psum[:, 5, c * P:(c + 1) * P], r2[:, c * P:(c + 1) * P], ident)
                    mm.then_inc(rT_done, 1)
                pe.wait_ge(vn_ready, j + 1)
                wait(pe, mix_read, j)
                g = 2 * i + u // 2
                for c in range(4):
                    mm = pe.matmul(psum[:, 5, c * P:(c + 1) * P], vn[:, c, :], wmt[:, bass.ds(g, 1), :].rearrange("p o t -> p (o t)"),
                                   start=True, stop=True)
                mm.then_inc(mix_done, 1)

            gate_tile(0, 0, first=True)
            for u in range(1, 4):
                gate_tile(0, u)
            with pe.Fori(1, 4) as i:
                for u in range(4):
                    gate_tile(i, u)
            pe.wait_ge(vs_ready, KG)
            wait(pe, vn_ready, KG)
            pe.wait_ge(mix_read, KG)
            pe.wait_ge(ln_done, GI["v"] + 1)
            for g in range(4):
                for c in range(4):
                    mm = pe.transpose(psum[0:NS, 4 + g, c * P:(c + 1) * P], vsn[:, 4 * g + c, :], ident)
                mm.then_inc(vsT_done, 1)

            def wo_tile(i, e, first=False):
                t = 2 * i + e
                wait(pe, sq_done, SQB["m_sgu"] + t - 1)
                for half in range(2):
                    unit(U_WO + 2 * t + half, half, e, range(half * KD, (half + 1) * KD), ush, usl, half == 0, half == 1,
                         ready=[(usl_ready, 0)] if first else None)

            pe.wait_ge(evac_sgu, 2 * KG)
            wo_tile(0, 0, first=True)
            wo_tile(0, 1)
            with pe.Fori(1, 4) as i:
                for e in range(2):
                    wo_tile(i, e)
            pe.wait_ge(cv_ready, 4)
            rms("m_sgu")

            def mlp(l):
                p = 1 + 2 * l
                par = U_UP[l] % 2
                pe.wait_ge(sq_done, SQB["m_attn" if l else "m_sgu"] + KD)
                two_units(U_UP[l], xh, xl, [(xl_ready, KD * p)])
                rms("x1" if l == 0 else "x3")

                def up(i, u):
                    q = 4 * i + u
                    pe.wait_ge(evac_up, NF * l + q - 1)
                    unit(U_UP[l] + q, (par + u) % 2, u % 2, range(KD), xh, xl, True, True)

                for u in range(2, 4):
                    up(0, u)
                with pe.Fori(1, NF // 4) as i:
                    for u in range(4):
                        up(i, u)

                g = "m_ffn0" if l == 0 else "m_ffn1"
                pd = U_DN[l] % 2

                def down(i, e, first=False):
                    t = 2 * i + e
                    if not first:
                        pe.wait_ge(sq_done, SQB[g] + t - 1)
                    for w, (k0, kc) in enumerate(DN_SPLIT):
                        unit(U_DN[l] + 4 * t + w, (pd + w) % 2, e, range(k0, k0 + kc), acth, actl, w == 0, w == 3,
                             ready=[(actl_ready, KF * l)] if first else None)

                pe.wait_ge(evac_up, NF * (l + 1))
                down(0, 0, first=True)
                pe.wait_ge(tails, NF * (l + 1))
                for b in range(5):
                    mm = pe.transpose(psum[0:2 * NF, 6 + b // 4, (b % 4) * P:(b % 4 + 1) * P],
                                      cs[:, :, :].rearrange("p k f -> p (k f)")[:, b * 2 * NF:(b + 1) * 2 * NF], ident)
                mm.then_inc(csT_done, 1)
                down(0, 1, first=False)
                with pe.Fori(1, 4) as i:
                    for e in range(2):
                        down(i, e)
                pe.wait_ge(csn_ready, l + 1)
                rms(g)

            mlp(0)

            pe.wait_ge(sq_done, SQB["m_ffn0"] + KD)
            two_units(U_KV, xkh, xkl, [(xkl_ready, 0)])
            rms("x2")
            pe.wait_ge(evac_kv, 1)
            unit(U_KV + 2, (U_KV + 2) % 2, 0, range(KD), xkh, xkl, True, True)
            for t in range(KQ):
                if t == 0:
                    pe.wait_ge(evac_kv, 2)
                elif t == 1:
                    pe.wait_ge(evac_kv, 3)
                else:
                    pe.wait_ge(evac_dq, t - 1)
                unit(U_DQ + t, (U_DQ + t) % 2, (3 + t) % 2, range(KD), xh, xl, True, True, ready=[(xl_ready, 2 * KD)] if t == 0 else None)
                if t == 0:
                    rms("kv")
            pe.wait_ge(evac_kv, 3)
            for b in range(2):
                mm = pe.matmul(psum[:, 4 + b, 0:HB], perm, krr[:, b * HB:(b + 1) * HB], start=True, stop=True)
            mm.then_inc(rotk_done, 1)
            rms("cq")
            for t in range(12):
                n = U_UQ + t // 2
                if t == 0:
                    pe.wait_ge(evac_dq, 3)
                elif t == 1:
                    pe.wait_ge(evac_dq, 4)
                else:
                    pe.wait_ge(evac_uq, t - 1)
                slot = (7 + t) % 2
                pe.wait_ge(w_low, n + 1)
                for k in range(KQ):
                    if t == 0:
                        pe.wait_ge(cql_ready, k + 1)
                    mm = product(n, slot, n % 2, k, (t % 2) * KQ + k, cqh, cql, k == 0, k == KQ - 1)
                if t % 2:
                    mm.then_inc(mm_done, 1)
                else:
                    mm.then_inc(uq_half, 1)
            for t in range(4):
                pe.wait_ge(evac_uq, 9 + t)
                if t >= 2:
                    pe.wait_ge(rotq_step, 2 * t - 2)
                else:
                    pe.wait_ge(evac_uq, 11 + t)
                slot = (7 + t) % 2
                for b in range(2):
                    mm = pe.matmul(psum[:, 2 * slot + b, 0:HB], perm, qrr[:, t, b * HB:(b + 1) * HB], start=True, stop=True)
                mm.then_inc(rotq_done, 1)

            pe.wait_ge(d_uk, 32)
            pe.wait_ge(rotk_step, 2)
            pe.wait_ge(ln_done, GI["cq"] + 1)
            for h in range(H):
                for c in range(KC):
                    mm = pe.transpose(psum[:, 4 + h // 2, (h % 2) * CL + c * P:(h % 2) * CL + (c + 1) * P], uk[:, c, h * P:(h + 1) * P], ident)
                if h % 2:
                    mm.then_inc(ukT_done, 1)
            pe.wait_ge(rotq_step, 8)
            pe.wait_ge(ukt_ready, 4)
            for c in range(KC):
                for h in range(H):
                    mm = pe.matmul(psum[:, 0, (c * H + h) * NS:(c * H + h + 1) * NS], ukt[:, h, c * P:(c + 1) * P], qn[:, h, SEQ:T],
                                   start=True, stop=True)
            mm.then_inc(ql_done, 1)
            for e in range(2):
                mm = pe.matmul(psum[0:ROPE, 1, e * 32:(e + 1) * 32], ident[:, e * ROPE:(e + 1) * ROPE], qr[:, :, SEQ:T],
                               start=True, stop=True)
            mm.then_inc(qsel_done, 1)
            def new_rows(c):
                cols, t0, bank = (P, (c - 1) * P, 4 + c % 2) if c else (NS, SEQ, 4)
                for k in range(KC):
                    pe.transpose(psum[0:cols, bank, k * P:(k + 1) * P], ckt[:, k, t0:t0 + cols], ident)
                pe.transpose(psum[0:cols, bank, CL:CL + ROPE], krt[0:ROPE, t0:t0 + cols], ident[0:ROPE, 0:ROPE]).then_inc(nT_done, 1)

            pe.wait_ge(ckt_ready, KC)
            new_rows(0)
            pe.wait_ge(qc_ready, 2)
            for s in range(NS):
                for c in range(3):
                    rows = P if c < 2 else ROPE
                    r = ckt[:, c, SEQ + s:SEQ + s + 1] if c < 2 else krt[0:ROPE, SEQ + s:SEQ + s + 1]
                    mm = pe.matmul(psum[0:H, 2, s:s + 1], qc[0:rows, c, s * H:(s + 1) * H], r, start=(c == 0), stop=(c == 2))
            mm.then_inc(sn_done, 1)
            pe.wait_ge(pick_ready, 1)
            pe.wait_ge(n_ready, 1)
            pe.wait_ge(sn_ready, 1)
            for s in range(NS):
                mm = pe.matmul(psum[0:H, s // 2, (s % 2) * CL:(s % 2 + 1) * CL], pick[0:NS, s, :], cksn[0:NS, 0:CL], start=True, stop=True)
            mm.then_inc(ckb_done, 1)

            def turn(g, b):
                m = 5 * g + b
                if b == 0:
                    pe.wait_ge(c_low, g + 1)
                if m >= 3:
                    g0, b0 = (m - 3) // 5, (m - 3) % 5
                    if b0 % 2:
                        pe.wait_ge(kt_v, 2 * g0 + b0 // 2 + 1)
                    else:
                        pe.wait_ge(kt_a, 3 * g0 + b0 // 2 + 1)
                for j in range(CH):
                    if b == 2:
                        src = kr2[:, g % 2, j, :]
                    else:
                        src = (lat_h if b < 2 else lat_l)[:, g % RING, j, (b % 3) * P:(b % 3 + 1) * P]
                    mm = pe.transpose(psum[:, 4 + m % 3, j * P:(j + 1) * P].bitcast(F32R), src, ident_r[:, :])
                mm.then_inc(cT_done, 1)

            TERMS = [(qh, 0, 0), (ql, 0, 0), (qh, 1, 1), (ql, 1, 1), (qh, 2, 2), (ql, 2, 2), (qh, 0, 3), (qh, 1, 4)]

            def score(g, i):
                s, c = g // NCH, g % NCH
                if i == 0:
                    pe.wait_ge(kt_a, 3 * g + 3)
                    pe.wait_ge(kt_v, 2 * g + 2)
                    wait(pe, e_done, NCH * (s - 1) + c + 1 if s else 0)
                q, k, b = TERMS[i]
                mm = pe.matmul(psum[0:H, c, :], q[:, k, s * H:(s + 1) * H], kt[g % 2][:, b, :], start=(i == 0), stop=(i == 7))
                if i == 7:
                    mm.then_inc(sc_done, 1)

            def turn_exps(s):
                pe.wait_ge(e_done, NCH * (s + 1))
                if s:
                    pe.wait_ge(pts_l, s)
                for b in range(NPG):
                    mm = pe.transpose(psum[:, 7, b * H:(b + 1) * H], ps_sb[0:H, b * P:(b + 1) * P], ident[0:H, 0:H])
                mm.then_inc(pT_done, 1)

            def weigh(s):
                pe.wait_ge(pts_l, s + 1)
                pe.wait_ge(dg_ready, s + 1)
                wait(pe, osn_ready, s)
                out = psum[0:PW, 7, CL:2 * CL]
                for j in range(NPG):
                    slot = (s * NCH + j // CH) % RING
                    for lat in (lat_h, lat_l):
                        mm = pe.matmul(out, pts[:, j, :], lat[:, slot, j % CH, :], start=(j == 0 and lat is lat_h),
                                       stop=(j == NPG - 1 and lat is lat_l))
                    if j == 0:
                        pe.matmul(psum[0:H, 7, CL:2 * CL], dg[0:H, :], ckb[0:H, s, :], start=False, stop=False)
                mm.then_inc(pv_done, 1)

            def turn_output(s):
                pe.wait_ge(osn_ready, s + 1)
                pe.wait_ge(foldr_ready, s + 1)
                for c in range(KC):
                    mm = pe.matmul(psum[:, 7, P + (c * NS + s) * H:P + (c * NS + s + 1) * H], osn[0:PW, c * P:(c + 1) * P],
                                   fold_r[0:PW, :], start=True, stop=True)
                mm.then_inc(olp_done, 1)

            pe.wait_ge(idr_ready, 1)
            pe.wait_ge(ql_ready, 2)
            pe.wait_ge(ckb_ready, 1)
            for g in range(NG + 4):
                c, s = g % NCH, g // NCH
                if g <= NG:
                    if g < NG:
                        turn(g, 0)
                        turn(g, 1)
                    for b in range(2, 6):
                        if g and c != 1:
                            score(g - 1, 2 * b - 4)
                            score(g - 1, 2 * b - 3)
                        if b < 5 and g < NG:
                            turn(g, b)
                    if c == 1:
                        for i in range(8):
                            score(g - 1, i)
                if s:
                    if c == 1:
                        turn_exps(s - 1)
                    elif c == 2:
                        weigh(s - 1)
                    elif c == 3:
                        turn_output(s - 1)
            pe.wait_ge(olT_ready, 1)
            for h in range(H):
                for c in range(KC):
                    mm = pe.matmul(psum[:, 0, h * NS:(h + 1) * NS], uv[:, c, h * P:(h + 1) * P], olT[:, c, h, :],
                                   start=(c == 0), stop=(c == KC - 1))
            mm.then_inc(os_done, 1)

            for g in range(16):
                bank = 4 + g % 4
                if g < 4:
                    pe.wait_ge(kt_a, 3 * NG)
                    pe.wait_ge(kt_v, 2 * NG)
                elif g % 2:
                    pe.wait_ge(kv_read_a, (g - 4) // 2 + 1)
                else:
                    pe.wait_ge(kv_read_v, (g - 4) // 2 + 1)
                for c in range(KC):
                    if g < 8:
                        lw, r = uk[:, c, g * P:(g + 1) * P], ckt[:, c, 0:SEQ]
                    else:
                        tk, hf = (g - 8) // 2, g % 2
                        lw, r = ckt[:, c, tk * P:(tk + 1) * P], uv[:, c, hf * 512:(hf + 1) * 512]
                    mm = pe.matmul(psum[:, bank, :], lw, r, start=(c == 0), stop=(c == KC - 1))
                mm.then_inc(kv_done, 1)
            for c in range(1, 5):
                if c == 1:
                    pe.wait_ge(kv_read_v, 7)
                    pe.wait_ge(kv_read_a, 7)
                else:
                    pe.wait_ge(n_ready, c - 1 if c > 2 else 1)
                new_rows(c)

            pe.wait_ge(os_ready, 1)
            pe.wait_ge(n_ready, 5)
            pe.wait_ge(kv_read_v, 8)
            pe.wait_ge(kv_read_a, 8)

            def scores(g):
                h, b = g // 4, g % 4
                if g >= 4:
                    pe.wait_ge(p_exp, g - 3)
                n = (b + 1) * P
                lo = (h % 2) * ROPE
                pe.matmul(psum[:, g % 4, 0:n], qn[:, h, b * P:(b + 1) * P], kn[:, h, 0:n], start=True, stop=False)
                pe.matmul(psum[:, g % 4, 0:n], qr[lo:lo + ROPE, h // 2, b * P:(b + 1) * P], krt[lo:lo + ROPE, 0:n],
                          start=False, stop=True).then_inc(s_done, 1)

            def turn_probs(g):
                h, b = g // 4, g % 4
                pe.wait_ge(p_norm, g + 1)
                if g >= 2:
                    pe.wait_ge(ppt_ready, g - 1)
                for j in range(b + 1):
                    mm = pe.transpose(psum[:, 4 + g % 2, j * P:(j + 1) * P], pp[:, g % 2, j * P:(j + 1) * P], ident)
                mm.then_inc(ppT_done, 1)

            def values(h):
                pe.wait_ge(ppt_ready, 4 * h + 4)
                if h >= 2:
                    pe.wait_ge(o_ready, h - 1)
                for j in range(4):
                    mm = pe.matmul(psum[:, 6 + h % 2, j * P:SEQ], v[:, j, h * P:(h + 1) * P], ppt[:, h % 2, j, j * P:SEQ],
                                   start=(j == 0), stop=(j == 3))
                mm.then_inc(ov_done, 1)

            for g in range(4 * H + 3):
                if g < 4 * H:
                    scores(g)
                if 2 <= g < 4 * H + 2:
                    turn_probs(g - 2)
                if g >= 6 and (g - 6) % 4 == 0:
                    values((g - 6) // 4)

            pe.wait_ge(p_exp, 4 * H)
            for t in range(KD):
                if t >= 2:
                    pe.wait_ge(sq_done, SQB["m_attn"] + t - 1)
                unit(U_O + t, (U_O + t) % 2, t % 2, range(KD), xh, xl, True, True, ready=[(ol_ready, 0)] if t == 0 else None)
            pe.wait_ge(o_ready, H)
            rms("m_attn")

            mlp(1)

            for c in range(5):
                cols = P if c < 4 else NS
                if c == 0:
                    pe.wait_ge(x_new, 4 * KD)
                if c >= 2:
                    pe.wait_ge(y_ready_v, c - 1)
                    pe.wait_ge(y_ready_a, c - 1)
                for t in range(KD):
                    mm = pe.transpose(psum[0:cols, 2 * (c % 2) + t // 4, (t % 4) * P:(t % 4 + 1) * P], x[:, t, c * P:c * P + cols], ident)
                mm.then_inc(yT_done, 1)

        @block.scalar
        def _(act):
            def fixed_wait():
                act.wait_ge(memset_done, 1)

            def split(n, slot4, slot2, stage_value):
                act.wait_ge(d_stage[slot4], stage_value)
                wait(act, mm_done, n - 1)
                act.activation(wh[:, slot2, :], ws[:, slot4, :], ACT.Copy).then_inc(w_high, 1)

            def ahead(base, per, i, u):
                m = base + u + 2
                n = m + per * i
                split(n, m % STAGES, m % 2, staged(m) + 16 * (per // STAGES) * i)

            def ahead_static(n):
                if n + 2 < U_END:
                    split(n + 2, (n + 2) % STAGES, n % 2, staged(n + 2))

            def rms(name, dst):
                g = GI[name]
                act.wait_ge(ss_done, g + 1)
                act.activation(halves(dst[:, :]), psum[:, 6:8, 0:HB], ACT.Ln, bias=eps[:, 0:1], scale=1.0 / GROUPS_SQ[g][2]).then_inc(ln_done, 1)
                act.wait_ge(ln_done, g + 1)
                act.activation(dst[:, :], dst[:, :], ACT.Exp, scale=-0.5).then_inc(r_ready, 1)

            def square(src, name, t, slot):
                wait(act, sq_added, SQB[name] + t - 1)
                out = sq[:, slot, :]
                act.activation(halves(out) if len(src.shape) == 3 else out, src, ACT.Square).then_inc(sq_done, 1)

            def update(p):
                name = f"x{p}"
                for t in range(KD):
                    if p:
                        act.wait_ge(x_new, KD * (p - 1) + t + 1)
                    else:
                        act.wait_ge(xin_v, t + 1)
                        act.wait_ge(xin_s, t + 1)
                        if t == 0:
                            act.wait_ge(pack_ready, 1)
                    if p == 2:
                        act.activation(xkh[:, t, :], x[:, t, :], ACT.Copy, scale=pt[:, G_KVIN + t:G_KVIN + t + 1]).then_inc(xkh_ready, 1)
                    else:
                        act.activation(xh[:, t, :], x[:, t, :], ACT.Copy, scale=pt[:, PRE[p] + t:PRE[p] + t + 1]).then_inc(xh_ready, 1)
                    square(x[:, t, :], name, t, t % 2)
                if p == 2:
                    for t in range(KD):
                        act.activation(xh[:, t, :], x[:, t, :], ACT.Copy, scale=pt[:, PRE[p] + t:PRE[p] + t + 1]).then_inc(xh_ready, 1)

            def raw(name, t, slot, m_dst):
                fixed_wait()
                act.activation(halves(m_dst), acc(slot), ACT.Copy).then_inc(m_ready, 1)
                square(acc(slot), name, t, slot % 2)

            for k, (src, r0, b, lo, n) in enumerate(PACK):
                act.dma_start(pn[lo:lo + n, b, :], rows_of(a[src] if len(a[src].shape) > 1 else a[src].rearrange("(o k) -> o k", o=1))[r0:r0 + n, :]).then_inc(
                    d_pack0 if b < 4 else d_pack1, 16)
            act.dma_start(wn[:, :, :], a["w_s"][0].rearrange("g t s -> t g s")).then_inc(d_gate, 16)
            act.dma_start(bsb[:, :, :], a["b_s"][0].partition_broadcast(P)).then_inc(d_bc, 16)
            act.dma_start(w00[:, :], a["w_s"][0, :, 0, 0].partition_broadcast(P), allow_slow_non_contiguous=True).then_inc(d_bc, 16)

            act.wait_ge(packT_done, 1)
            act.activation(pt[:, 0:512], psum[:, 4, :], ACT.Copy).then_inc(pack_ready, 1)
            for t in range(KD):
                act.wait_ge(xT_done, t + 1)
                act.activation(x[:, t, SEQ:T], psum[:, 2 * (t % 2) + 1, 0:NS], ACT.Copy).then_inc(xin_s, 1)
            split(0, 0, 0, staged(0))
            split(1, 1, 1, staged(1))
            update(0)

            def value_tile(i, u):
                j = 4 * i + u
                wait(act, sq_added, SQB["v"] + j - 1)
                act.wait_ge(evac_sgu, j + 1)
                fixed_wait()
                act.activation(zv[:, bass.ds(j, 1), :].rearrange("p o t -> p (o t)"), ut[:, u % 2, :], ACT.Gelu).then_inc(z_done, 1)
                fixed_wait()
                act.wait_ge(z_done, j + 1)
                act.activation(sq[:, u % 2, :], zv[:, bass.ds(j, 1), :].rearrange("p o t -> p (o t)"), ACT.Square).then_inc(sq_done, 1)

            for u in range(4):
                ahead(U_V, 4, 0, u)
                if u == 0:
                    rms("x0", r1)
                value_tile(0, u)
            for g in range(1, 4):
                act.wait_ge(packT_done, g + 1)
                n = min(512, C_END - 512 * g)
                act.activation(pt[:, 512 * g:512 * g + n], psum[:, 4 + g % 2, 0:n], ACT.Copy).then_inc(pack_ready, 1)
            with act.Fori(1, 4) as i:
                for u in range(4):
                    ahead(U_V, 4, i, u)
                    value_tile(i, u)

            def gate_tile(i, u, first=False):
                j = 4 * i + u
                if first:
                    ahead(U_U, 4, i, u)
                    rms("v", r2)
                    act.wait_ge(rT_done, 1)
                    act.activation(rn[:, 0:4], psum[:, 5, :].rearrange("p (c t) -> p c t", c=4)[:, :, 0], ACT.Copy).then_inc(rn_ready, 1)
                    act.wait_ge(rn_ready, 1)
                act.wait_ge(zT_done, j + 1)
                wait(act, mix_done, j)
                for c in range(4):
                    mm = act.activation(vn[:, c, :], psum[:, 4, c * P:(c + 1) * P], ACT.Copy, scale=rn[:, c:c + 1])
                mm.then_inc(vn_ready, 1)
                if not first:
                    ahead(U_U, 4, i, u)
                act.wait_ge(evac_sgu, KG + j + 1)
                wait(act, us_prod, j)
                act.activation(ut[:, 1, :], ut[:, 0, :], ACT.Gelu).then_inc(u_gelu, 1)
                act.wait_ge(us_prod, j + 1)
                fixed_wait()
                act.activation(ush[:, bass.ds(j, 1), :].rearrange("p o t -> p (o t)"), sq[:, 0, :], ACT.Copy).then_inc(ush_ready, 1)

            gate_tile(0, 0, first=True)
            for u in range(1, 4):
                gate_tile(0, u)
            with act.Fori(1, 4) as i:
                for u in range(4):
                    gate_tile(i, u)

            def wo(i):
                for e in range(2):
                    for half in range(2):
                        ahead(U_WO, 4, i, 2 * e + half)
                    t = 2 * i + e
                    act.wait_ge(mm_done, U_WO + 2 * t + 2)
                    raw("m_sgu", t, e, m_raw[:, bass.ds(t, 1), :].rearrange("p o t -> p (o t)"))
            with act.Fori(0, 4) as i:
                wo(i)
            rms("m_sgu", r2)
            update(1)

            def mlp(l):
                def high_product(j):
                    act.wait_ge(prod_done, KF * l + j + 1)
                    fixed_wait()
                    act.activation(acth[:, bass.ds(j, 1), :].rearrange("p o t -> p (o t)"), pr[:, :], ACT.Copy).then_inc(acth_ready, 1)

                def tile(i, u, first=False):
                    ahead(U_UP[l], 4, i, u)
                    if first:
                        rms("x1" if l == 0 else "x3", r1)
                    q, j = 4 * i + u, 2 * i + u // 2
                    if u % 2 == 0:
                        if not first:
                            high_product(j - 1)
                        act.wait_ge(conv_done, NF * l + q + 1)
                        act.activation(cc[:, 0, :], cc[:, 0, :], ACT.Gelu_apprx_tanh).then_inc(gelu_done, 1)

                for u in range(4):
                    tile(0, u, first=(u == 0))
                with act.Fori(1, NF // 4) as i:
                    for u in range(4):
                        tile(i, u)
                high_product(KF - 1)

                g = "m_ffn0" if l == 0 else "m_ffn1"

                def down(i, e, guard=False):
                    t = 2 * i + e
                    for w in range(4):
                        if guard:
                            ahead_static(U_DN[l] + 4 * t + w)
                        else:
                            ahead(U_DN[l], 8, i, 4 * e + w)
                    act.wait_ge(mm_done, U_DN[l] + 4 * t + 4)
                    raw(g, t, e, m_raw[:, bass.ds(t, 1), :].rearrange("p o t -> p (o t)") if not isinstance(t, int) else m_raw[:, t, :])

                down(0, 0)
                act.wait_ge(csT_done, l + 1)
                act.activation(csn[0:2 * NF, 0:4, :].rearrange("p a b -> p (a b)"), psum[0:2 * NF, 6, :], ACT.Copy)
                act.activation(csn[0:2 * NF, 4, :], psum[0:2 * NF, 7, 0:P], ACT.Copy).then_inc(csn_ready, 1)
                down(0, 1)
                with act.Fori(1, 3) as i:
                    for e in range(2):
                        down(i, e)
                for e in range(2):
                    down(3, e, guard=True)
                rms(g, r2)

            mlp(0)
            update(2)

            ahead_static(U_KV)
            rms("x2", r1)
            for t in range(KC):
                act.wait_ge(evac_kv, t + 1)
                square(kvr[:, t, :], "kv", t, t % 2)
            ahead_static(U_KV + 1)
            ahead_static(U_KV + 2)
            ahead_static(U_DQ)
            rms("kv", r2)
            for t in range(KQ):
                act.wait_ge(evac_dq, t + 1)
                square(cqr[:, t, :], "cq", t, t % 2)
                act.activation(cqh[:, t, :], cqr[:, t, :], ACT.Copy, scale=pt[:, G_Q + t:G_Q + t + 1]).then_inc(cqh_ready, 1)
                if t < KQ - 1:
                    ahead_static(U_DQ + t + 1)
            act.wait_ge(ckt_ready, KC)
            rms("cq", r2)
            for j in range(4):
                ahead_static(U_UQ + j)
            act.wait_ge(d_uk, 32)
            for g in range(4):
                act.wait_ge(ukT_done, g + 1)
                if g == 0:
                    act.wait_ge(mm_done, U_UQ + 6)
                act.activation(ukt[:, 2 * g:2 * g + 2, :].rearrange("p a b -> p (a b)"), psum[:, 4 + g, :], ACT.Copy).then_inc(ukt_ready, 1)
            def new_rows(c):
                act.wait_ge(nT_done, c + 1)
                if c > 2:
                    act.wait_ge(okn_sent[(c - 1) % 2], 32)
                if c:
                    act.activation(okn[:, (c - 1) % 2, :], psum[:, 4 + c % 2, 0:320], ACT.Copy).then_inc(n_ready, 1)
                else:
                    act.activation(cksn[0:NS, :], psum[0:NS, 4, 0:320], ACT.Copy).then_inc(n_ready, 1)

            act.wait_ge(evac_uq, 12)
            act.activation(ident_r[:, :], ident, ACT.Copy).then_inc(idr_ready, 1)
            new_rows(0)
            act.wait_ge(qc_ready, 2)
            act.activation(qh[:, 0:2, :], qc[:, 0:2, :], ACT.Copy)
            act.activation(qh[0:ROPE, 2, :], qc[0:ROPE, 2, :], ACT.Copy)
            act.activation(qh[ROPE:P, 2, :], qc[0:ROPE, 2, :], ACT.Copy).then_inc(qh_ready, 1)
            act.wait_ge(ckb_done, 1)
            act.activation(ckb[0:H, :, :].rearrange("p a b -> p (a b)"), psum[0:H, 0:4, :].rearrange("p a b -> p (a b)"), ACT.Copy).then_inc(ckb_ready, 1)
            act.activation(pts[:, :, H:32], cst[:, 0:NPG * (32 - H)].rearrange("p (a b) -> p a b", a=NPG), ACT.Copy, scale=0.0)

            def high(g):
                act.wait_ge(d_cn[g % CN_SLOTS], 16 * 2 * CH * (g // CN_SLOTS + 1))
                if g >= 2:
                    act.wait_ge(cT_done, 5 * (g - 2) + 3)
                if g >= RING:
                    act.wait_ge(pv_done, g // NCH - 1)
                src = cn[:, g % CN_SLOTS, :, :]
                act.activation(lat_h[:, g % RING, :, :], src[:, :, 0:CL], ACT.Copy)
                act.activation(kr2[:, g % 2, :, 0:ROPE], src[:, :, CL:CL + ROPE], ACT.Copy).then_inc(c_high, 1)

            def turned_block(g, b):
                act.wait_ge(cT_done, 5 * g + b + 1)
                if g >= 2:
                    act.wait_ge(sc_done, g - 1)
                act.activation(kt[g % 2][:, b, :], psum[:, 4 + (5 * g + b) % 3, :], ACT.Copy).then_inc(kt_a, 1)

            def exps(s):
                act.wait_ge(neg_ready, s + 1)
                wait(act, pT_done, s)
                neg = smp[0:H, 10 * NS + s:10 * NS + s + 1]
                for c in range(NCH):
                    act.activation(ps_sb[0:H, c * 512:(c + 1) * 512], psum[0:H, c, :], ACT.Exp, bias=neg, scale=SCALE,
                                   accum_out=smp[0:H, 5 * NS + 5 * s + c:5 * NS + 5 * s + c + 1]).then_inc(e_done, 1)
                act.activation(smp[0:H, 5 * NS + 5 * s + 4:5 * NS + 5 * s + 5], smp[0:H, 5 * s + 4:5 * s + 5], ACT.Exp, bias=neg,
                               scale=SCALE).then_inc(own_ready, 1)

            act.wait_ge(mm_done, U_O)
            act.wait_ge(w_low, U_O)
            act.wait_ge(rotq_step, 8)
            high(0)
            for g in range(NG + 4):
                c, s = g % NCH, g // NCH
                if s and c == 2:
                    act.wait_ge(pT_done, s)
                    wait(act, pv_done, s - 1)
                    act.activation(pts[:, :, 0:H], psum[:, 7, 0:P].rearrange("p (a b) -> p a b", b=H), ACT.Copy).then_inc(pts_h, 1)
                if g < NG:
                    turned_block(g, 0)
                    if g + 1 < NG:
                        high(g + 1)
                    turned_block(g, 2)
                    turned_block(g, 4)
                if s and c == 0:
                    exps(s - 1)
                if s and c == 3:
                    act.wait_ge(pv_done, s)
                    wait(act, olp_done, s - 1)
                    act.activation(osn[0:PW, :], psum[0:PW, 7, CL:2 * CL], ACT.Copy).then_inc(osn_ready, 1)
            act.wait_ge(sc_done, NG)
            act.wait_ge(pv_done, NS)
            split(U_O, U_O % STAGES, U_O % 2, staged(U_O))
            split(U_O + 1, (U_O + 1) % STAGES, (U_O + 1) % 2, staged(U_O + 1))
            for g in range(1, 16, 2):
                act.wait_ge(kv_done, g + 1)
                dst = kn[:, g, :] if g < 8 else v[:, (g - 8) // 2, 512:1024]
                act.activation(dst, psum[:, 4 + g % 4, :], ACT.Copy).then_inc(kv_read_a, 1)
            for c in range(1, 5):
                new_rows(c)

            def turned(g):
                h, b = g // 4, g % 4
                act.wait_ge(ppT_done, g + 1)
                wait(act, ov_done, h - 1)
                act.activation(ppt[:, h % 2, 0:b + 1, b * P:(b + 1) * P], psum[:, 4 + g % 2, 0:(b + 1) * P].rearrange("p (j t) -> p j t", t=P),
                               ACT.Copy).then_inc(ppt_ready, 1)

            for g in range(4 * H):
                b = g % 4
                n = (b + 1) * P
                act.wait_ge(s_neg, g + 1)
                if g >= 2:
                    act.wait_ge(ppT_done, g - 1)
                act.activation(pp[:, g % 2, 0:n], psum[:, g % 4, 0:n], ACT.Exp, bias=small[:, 8 + g % 2:9 + g % 2], scale=SCALE,
                               accum_out=small[:, 10 + g % 2:11 + g % 2]).then_inc(p_exp, 1)
                if g >= 2:
                    turned(g - 2)
            turned(4 * H - 2)
            turned(4 * H - 1)
            for h in range(H):
                act.wait_ge(o_ready, h + 1)
                if h == 0:
                    act.wait_ge(s_done, 4 * H)
                    act.wait_ge(os_ready, 1)
                act.activation(xh[:, h, :], o[:, h, :], ACT.Copy).then_inc(oh_ready, 1)
            for t in range(KD):
                ahead_static(U_O + t)
                act.wait_ge(mm_done, U_O + t + 1)
                raw("m_attn", t, t % 2, m_attn[:, t, :])
            rms("m_attn", r2)
            update(3)
            mlp(1)
            for c in range(5):
                rows = P if c < 4 else NS
                act.wait_ge(yT_done, c + 1)
                act.activation(yn[0:rows, c, 512:1024], psum[0:rows, 2 * (c % 2) + 1, :], ACT.Copy).then_inc(y_ready_a, 1)

        @block.vector
        def _(dve):
            def split(n, slot4, slot2):
                dve.wait_ge(w_high, n + 1)
                dve.tensor_tensor(wl[:, slot2, :], ws[:, slot4, :], f32(wh[:, slot2, :]), ALU.subtract).then_inc(w_low, 1)

            def ahead(base, per, i, u):
                m = base + u + 2
                split(m + per * i, m % STAGES, m % 2)

            def ahead_static(n):
                if n + 2 < U_END:
                    split(n + 2, (n + 2) % STAGES, n % 2)

            def low(p, t):
                if p == 2:
                    dve.wait_ge(xkh_ready, t + 1)
                    dve.scalar_tensor_tensor(out=xkl[:, t, :], in0=x[:, t, :], scalar=pt[:, G_KVIN + t:G_KVIN + t + 1], in1=f32(xkh[:, t, :]),
                                             op0=ALU.mult, op1=ALU.subtract).then_inc(xkl_ready, 1)
                else:
                    low_mix(p, t)

            def low_mix(p, t):
                dve.wait_ge(xh_ready, KD * p + t + 1)
                dve.scalar_tensor_tensor(out=xl[:, t, :], in0=x[:, t, :], scalar=pt[:, PRE[p] + t:PRE[p] + t + 1], in1=f32(xh[:, t, :]),
                                         op0=ALU.mult, op1=ALU.subtract).then_inc(xl_ready, 1)

            def update(p, m):
                dve.wait_ge(r_ready, GI[["", "m_sgu", "m_ffn0", "m_attn", "m_ffn1"][p]] + 1)
                if p % 2 == 0:
                    dve.wait_ge(csn_sent, 16 * 9 * (p // 2))
                for t in range(KD):
                    k = KD * (p - 1) + t
                    wait(dve, x_new, k - 1)
                    dve.scalar_tensor_tensor(out=ut[:, t % 2, :], in0=m[:, t, :], scalar=pt[:, POST[p] + t:POST[p] + t + 1], in1=r2[:, :],
                                             op0=ALU.mult, op1=ALU.mult).then_inc(u_mul, 1)
                    dve.wait_ge(u_mul, k + 1)
                    dve.tensor_tensor(x[:, t, :], x[:, t, :], ut[:, t % 2, :], ALU.add).then_inc(x_new, 1)
                    if p < 4 and t:
                        low(p, t - 1)
                if p < 4:
                    low(p, KD - 1)
                if p == 2:
                    for t in range(KD):
                        low_mix(p, t)

            dve.memset(ones[:, :], 1.0)
            dve.memset(eps[:, :], EPS).then_inc(memset_done, 1)
            for t in range(KD):
                dve.wait_ge(xT_done, t + 1)
                dve.tensor_copy(x[:, t, 0:SEQ], psum[:, 2 * (t % 2), :]).then_inc(xin_v, 1)
            split(0, 0, 0)
            split(1, 1, 1)
            for t in range(KD):
                low(0, t)
                add_squares(dve, "x0", t, t % 2)

            def value_tile(i, u, first=False):
                j = 4 * i + u
                ahead(U_V, 4, i, u)
                dve.wait_ge(mm_done, U_V + j + 1)
                if first:
                    dve.wait_ge(r_ready, 1)
                wait(dve, z_done, j - 1)
                dve.tensor_tensor(halves(ut[:, u % 2, :]), acc(u % 2), halves(r1[:, :]), ALU.mult).then_inc(evac_sgu, 1)
                add_squares(dve, "v", j, u % 2)

            for u in range(4):
                value_tile(0, u, first=(u == 0))
            dve.wait_ge(gT_done, 1)
            dve.wait_ge(d_const, 16)
            for g in range(GROUPS):
                mm = dve.tensor_tensor(wmt[:, g, :], psum[:, 6 + g // 4, (g % 4) * P:(g % 4 + 1) * P], keep, ALU.mult)
            mm.then_inc(wm_ready, 1)
            with dve.Fori(1, 4) as i:
                for u in range(4):
                    value_tile(i, u)

            dve.wait_ge(z_done, KG)
            dve.tensor_copy(zs[:, :], zv[:, 0, :]).then_inc(zs_ready, 1)
            dve.wait_ge(d_bc, 32)

            def gate_tile(i, u, first=False, last=False):
                j, g = 4 * i + u, 2 * i + u // 2
                if not last:
                    dve.wait_ge(zT_done, j + 1)
                    dve.tensor_copy(zs[:, :], zv[:, bass.ds(j + 1, 1), :].rearrange("p o t -> p (o t)")).then_inc(zs_ready, 1)
                ahead(U_U, 4, i, u)
                if first:
                    dve.wait_ge(r_ready, GI["v"] + 1)
                dve.scalar_tensor_tensor(out=vsn[:, bass.ds(j, 1), :].rearrange("p o t -> p (o t)"),
                                         in0=zv[:, bass.ds(j, 1), SEQ:T].rearrange("p o t -> p (o t)"), scalar=pt[:, bass.ds(G_SGU + j, 1)],
                                         in1=r2[:, SEQ:T], op0=ALU.mult, op1=ALU.mult).then_inc(vs_ready, 1)
                dve.wait_ge(mm_done, U_U + j + 1)
                wait(dve, u_gelu, j)
                dve.tensor_tensor(halves(ut[:, 0, :]), acc(u % 2), halves(r1[:, :]), ALU.mult).then_inc(evac_sgu, 1)
                dve.wait_ge(vs_ready, j + 1)
                wait(dve, us_prod, j)
                dve.tensor_scalar(sT[:, SEQ:T], vsn[:, bass.ds(j, 1), :].rearrange("p o t -> p (o t)"), w00[:, bass.ds(g, 1)], bsb[:, bass.ds(g, 1), 0:1].rearrange("p o t -> p (o t)"),
                                  ALU.mult, ALU.add)
                dve.wait_ge(mix_done, j + 1)
                bias = bsb[:, bass.ds(g, 1), :].to_broadcast([P, 4, P])
                dve.scalar_tensor_tensor(out=sT[:, 0:SEQ].rearrange("p (c t) -> p c t", c=4), in0=psum[:, 5, :].rearrange("p (c t) -> p c t", c=4),
                                         scalar=pt[:, bass.ds(G_SGU + j, 1)], in1=bias, op0=ALU.mult, op1=ALU.add).then_inc(mix_read, 1)
                dve.wait_ge(mix_read, j + 1)
                dve.wait_ge(u_gelu, j + 1)
                wait(dve, usl_ready, j)
                dve.tensor_tensor(sq[:, 0, :], sT[:, :], ut[:, 1, :], ALU.mult).then_inc(us_prod, 1)
                dve.wait_ge(ush_ready, j + 1)
                dve.wait_ge(us_prod, j + 1)
                dve.tensor_tensor(usl[:, bass.ds(j, 1), :].rearrange("p o t -> p (o t)"), sq[:, 0, :],
                                  f32(ush[:, bass.ds(j, 1), :]).rearrange("p o t -> p (o t)"), ALU.subtract).then_inc(usl_ready, 1)

            gate_tile(0, 0, first=True)
            for u in range(1, 4):
                gate_tile(0, u)
            with dve.Fori(1, 3) as i:
                for u in range(4):
                    gate_tile(i, u)
            for u in range(4):
                gate_tile(3, u, last=(u == 3))
            for g in range(4):
                dve.wait_ge(vsT_done, g + 1)
                if g:
                    dve.wait_ge(cv_sent, 16 * g)
                dve.tensor_copy(cvo[0:NS, :, :].rearrange("p a b -> p (a b)"), psum[0:NS, 4 + g, :]).then_inc(cv_ready, 1)

            def wo(i):
                for e in range(2):
                    for half in range(2):
                        ahead(U_WO, 4, i, 2 * e + half)
                    add_squares(dve, "m_sgu", 2 * i + e, e)
            wo(0)
            with dve.Fori(1, 4) as i:
                wo(i)
            update(1, m_raw)

            def mlp(l):
                def low_product(j):
                    dve.wait_ge(acth_ready, KF * l + j + 1)
                    dve.wait_ge(prod_done, KF * l + j + 1)
                    dve.tensor_tensor(actl[:, bass.ds(j, 1), :].rearrange("p o t -> p (o t)"), pr[:, :],
                                      f32(acth[:, bass.ds(j, 1), :]).rearrange("p o t -> p (o t)"), ALU.subtract).then_inc(actl_ready, 1)

                def tile(i, u, first=False):
                    q, j = 4 * i + u, 2 * i + u // 2
                    f = (u % 2) * KF + j
                    Q, J, b = NF * l + q, KF * l + j, u % 2
                    dve.wait_ge(mm_done, U_UP[l] + q + 1)
                    if first:
                        dve.wait_ge(r_ready, GI["x1" if l == 0 else "x3"] + 1)
                        dve.wait_ge(zpad, 1 + l)
                        if l == 0:
                            dve.wait_ge(cv_sent, 16 * 4)
                        else:
                            dve.wait_ge(n_sent, 32)
                            for sent in okn_sent:
                                dve.wait_ge(sent, 64)
                    wait(dve, tails, Q - 1)
                    wait(dve, conv_done, Q - 1)
                    a_b = psum[:, 2 * b:2 * b + 2, :]
                    dve.tensor_tensor(ab[:, b, 2:2 + HB], a_b[:, 0, 0:HB], r1[:, 0:HB], ALU.mult)
                    dve.tensor_tensor(ab[:, b, 2 + HB:2 + SEQ], a_b[:, 1, 0:SEQ - HB], r1[:, HB:SEQ], ALU.mult)
                    dve.tensor_tensor(ab[:, b, 2 + SEQ:].rearrange("p (s k) -> p s k", k=3)[:, :, 2], a_b[:, 1, SEQ - HB:HB], r1[:, SEQ:T],
                                      ALU.mult).then_inc(evac_up, 1)
                    ahead(U_UP[l], 4, i, u)
                    if b == 0 and not first:
                        low_product(j - 1)
                    dve.wait_ge(evac_up, Q + 1)
                    dve.wait_ge(state_in, Q + 1)
                    wait(dve, prod_done, J)
                    w = [pt[:, bass.ds(conv_rows(l, k) + f, 1)] for k in range(3)]
                    bias = pt[:, bass.ds(C_CB + l * NF + f, 1)]
                    dve.tensor_scalar(cc[:, b, :], ab[:, b, 0:CW_], w[0], bias, ALU.mult, ALU.add).then_inc(conv_step, 1)
                    dve.wait_ge(conv_step, 2 * Q + 1)
                    dve.scalar_tensor_tensor(out=cc[:, b, :], in0=ab[:, b, 1:1 + CW_], scalar=w[1], in1=cc[:, b, :], op0=ALU.mult, op1=ALU.add)\
                       .then_inc(conv_step, 1)
                    dve.wait_ge(conv_step, 2 * Q + 2)
                    dve.scalar_tensor_tensor(out=cc[:, b, :], in0=ab[:, b, 2:2 + CW_], scalar=w[2], in1=cc[:, b, :], op0=ALU.mult, op1=ALU.add)\
                       .then_inc(conv_done, 1)
                    if b:
                        dve.wait_ge(gelu_done, J + 1)
                        dve.wait_ge(conv_done, Q + 1)
                        wait(dve, actl_ready, J)
                        wait(dve, acth_ready, J)
                        dve.tensor_tensor(pr[:, 0:SEQ], cc[:, 0, 0:SEQ], cc[:, 1, 0:SEQ], ALU.mult)
                        smp = [cc[:, e, SEQ:].rearrange("p (s k) -> p s k", k=3)[:, :, 2] for e in range(2)]
                        dve.tensor_tensor(pr[:, SEQ:T], smp[0], smp[1], ALU.mult).then_inc(prod_done, 1)

                for u in range(4):
                    tile(0, u, first=(u == 0))
                with dve.Fori(1, NF // 4) as i:
                    for u in range(4):
                        tile(i, u)
                low_product(KF - 1)
                g = "m_ffn0" if l == 0 else "m_ffn1"

                def down(i, e, guard=False):
                    t = 2 * i + e
                    for w in range(4):
                        if guard:
                            ahead_static(U_DN[l] + 4 * t + w)
                        else:
                            ahead(U_DN[l], 8, i, 4 * e + w)
                    add_squares(dve, g, t, e)

                down(0, 0)
                down(0, 1)
                with dve.Fori(1, 3) as i:
                    for e in range(2):
                        down(i, e)
                for e in range(2):
                    down(3, e, guard=True)

            mlp(0)
            update(2, m_raw)

            ahead_static(U_KV)
            dve.wait_ge(r_ready, GI["x2"] + 1)
            for t in range(KC):
                dve.wait_ge(mm_done, U_KV + t + 1)
                dve.tensor_tensor(halves(kvr[:, t, :]), acc(t), halves(r1[:, :]), ALU.mult).then_inc(evac_kv, 1)
            for t in range(KC):
                add_squares(dve, "kv", t, t % 2)
            ahead_static(U_KV + 1)
            dve.wait_ge(mm_done, U_KV + 3)
            dve.tensor_tensor(halves(krr[:, :]), acc(0), halves(r1[:, :]), ALU.mult).then_inc(evac_kv, 1)
            ahead_static(U_KV + 2)
            ahead_static(U_DQ)
            dve.wait_ge(r_ready, GI["kv"] + 1)
            for t in range(KC):
                dve.scalar_tensor_tensor(out=ckt[:, t, :], in0=kvr[:, t, :], scalar=pt[:, G_KV + t:G_KV + t + 1], in1=r2[:, :],
                                         op0=ALU.mult, op1=ALU.mult).then_inc(ckt_ready, 1)
            for t in range(KQ):
                dve.wait_ge(mm_done, U_DQ + t + 1)
                dve.tensor_tensor(halves(cqr[:, t, :]), acc((3 + t) % 2), halves(r1[:, :]), ALU.mult).then_inc(evac_dq, 1)
                add_squares(dve, "cq", t, t % 2)
                dve.wait_ge(cqh_ready, t + 1)
                dve.scalar_tensor_tensor(out=cql[:, t, :], in0=cqr[:, t, :], scalar=pt[:, G_Q + t:G_Q + t + 1], in1=f32(cqh[:, t, :]),
                                         op0=ALU.mult, op1=ALU.subtract).then_inc(cql_ready, 1)
                if t < KQ - 1:
                    ahead_static(U_DQ + t + 1)

            def rotate(dst, raw_, rot, tmp, done, step, n):
                dve.wait_ge(done, n + 1)
                dve.tensor_tensor(halves(tmp), rot, halves(sin), ALU.mult)
                dve.tensor_tensor(dst, raw_, cos, ALU.mult).then_inc(step, 1)
                dve.wait_ge(step, 2 * n + 1)
                dve.tensor_tensor(dst, dst, tmp, ALU.add).then_inc(step, 1)

            rotate(krt[:, :], krr[:, :], psum[:, 4:6, 0:HB], ut[:, 0, :], rotk_done, rotk_step, 0)
            dve.wait_ge(r_ready, GI["cq"] + 1)
            for t in range(12):
                if t % 2:
                    dve.wait_ge(mm_done, U_UQ + t // 2 + 1)
                else:
                    dve.wait_ge(uq_half, t // 2 + 1)
                dst = qn[:, t, :] if t < 8 else qrr[:, t - 8, :]
                dve.tensor_tensor(halves(dst), acc((7 + t) % 2), halves(r2[:, :]), ALU.mult).then_inc(evac_uq, 1)
                if t % 2 and t < 8:
                    ahead_static(U_UQ + t // 2)
            for t in range(4):
                dve.wait_ge(evac_uq, 12)
                wait(dve, rotq_step, 2 * t - 2)
                rotate(qr[:, t, :], qrr[:, t, :], acc((7 + t) % 2), ut[:, t % 2, :], rotq_done, rotq_step, t)

            dve.wait_ge(ql_done, 1)
            dve.wait_ge(qsel_done, 1)
            for c in range(KC):
                mm = dve.tensor_copy(qc[:, c, :].rearrange("p (s h) -> p s h", s=NS), psum[:, 0, c * 64:(c + 1) * 64].rearrange("p (h s) -> p s h", h=H))
            mm.then_inc(qc_ready, 1)
            for e in range(2):
                mm = dve.tensor_copy(qc[0:ROPE, 2, :].rearrange("p (s h e) -> p s h e", s=NS, e=2)[:, :, :, e],
                                     psum[0:ROPE, 1, e * 32:(e + 1) * 32].rearrange("p (h s) -> p s h", h=4))
            mm.then_inc(qc_ready, 1)
            dve.tensor_copy(pick[0:NS, :, :], ident[0:NS, 0:NS].rearrange("p (s o) -> p s o", o=1).to_broadcast([NS, NS, H])).then_inc(pick_ready, 1)
            dve.memset(fold[:, :], 0.0)
            dve.memset(smp[:, 12 * NS:13 * NS], 0.0).then_inc(fold_ready, 1)
            dve.wait_ge(fold_ready, 1)
            dve.tensor_copy(fold[0:H, :], ident[0:H, 0:H])
            dve.tensor_copy(fold[32:32 + H, :], ident[32:32 + H, 32:32 + H]).then_inc(fold_ready, 1)
            dve.wait_ge(sn_done, 1)
            dve.tensor_copy(smp[0:H, 0:5 * NS].rearrange("p (s k) -> p s k", k=5)[:, :, 4], psum[0:H, 2, 0:NS]).then_inc(sn_ready, 1)
            dve.wait_ge(qh_ready, 1)
            dve.tensor_tensor(ql[:, 0:2, :], qc[:, 0:2, :], f32(qh[:, 0:2, :]), ALU.subtract)
            dve.tensor_tensor(ql[0:ROPE, 2, :], qc[0:ROPE, 2, :], f32(qh[0:ROPE, 2, :]), ALU.subtract).then_inc(ql_ready, 1)
            dve.tensor_tensor(ql[ROPE:P, 2, :], f32(qh[ROPE:P, 2, :]), f32(qh[ROPE:P, 2, :]), ALU.subtract).then_inc(ql_ready, 1)

            def chunk_low(g):
                dve.wait_ge(c_high, g + 1)
                src = cn[:, g % CN_SLOTS, :, :]
                dve.tensor_tensor(lat_l[:, g % RING, :, :], src[:, :, 0:CL], f32(lat_h[:, g % RING, :, :]), ALU.subtract)
                dve.tensor_tensor(kr2[:, g % 2, :, ROPE:P], src[:, :, CL:CL + ROPE], f32(kr2[:, g % 2, :, 0:ROPE]), ALU.subtract).then_inc(c_low, 1)

            def turned_block(g, b):
                dve.wait_ge(cT_done, 5 * g + b + 1)
                if g >= 2:
                    dve.wait_ge(sc_done, g - 1)
                dve.tensor_copy(kt[g % 2][:, b, :], psum[:, 4 + (5 * g + b) % 3, :]).then_inc(kt_v, 1)

            def col(k, s):
                return smp[0:H, k * NS + s:k * NS + s + 1]

            chunk_low(0)
            dve.wait_ge(fold_ready, 2)
            for g in range(NG + 4):
                c, s = g % NCH, g // NCH
                if s and c == 2:
                    dve.wait_ge(pts_h, s)
                    dve.tensor_tensor(pts[:, :, 32:PW], psum[:, 7, 0:P].rearrange("p (a b) -> p a b", b=H), f32(pts[:, :, 0:H]),
                                      ALU.subtract).then_inc(pts_l, 1)
                if g < NG:
                    turned_block(g, 1)
                    if g + 1 < NG:
                        chunk_low(g + 1)
                    turned_block(g, 3)
                if 1 <= g <= NG:
                    s0, c0 = (g - 1) // NCH, (g - 1) % NCH
                    dve.wait_ge(sc_done, g)
                    dve.tensor_reduce(smp[0:H, 5 * s0 + c0:5 * s0 + c0 + 1], psum[0:H, c0, :], AX_X, ALU.max).then_inc(mx_done, 1)
                if s and c == 0:
                    dve.wait_ge(mx_done, NCH * s)
                    dve.tensor_reduce(col(12, s - 1), smp[0:H, 5 * (s - 1):5 * s], AX_X, ALU.max).then_inc(mx_all, 1)
                    dve.wait_ge(mx_all, s)
                    dve.tensor_scalar(col(10, s - 1), col(12, s - 1), -SCALE, None, ALU.mult).then_inc(neg_ready, 1)
                if s and c == 1:
                    dve.wait_ge(own_ready, s)
                    wait(dve, pv_done, s - 1)
                    dve.tensor_scalar(dg[0:H, :], ident[0:H, 0:H], smp[0:H, 5 * NS + 5 * s - 1:5 * NS + 5 * s], None, ALU.mult).then_inc(dg_ready, 1)
                    dve.tensor_reduce(col(11, s - 1), smp[0:H, 5 * NS + 5 * (s - 1):5 * NS + 5 * s], AX_X, ALU.add).then_inc(tot_ready, 1)
                    dve.wait_ge(tot_ready, s)
                    dve.reciprocal(smp[32:32 + H, 12 * NS + s - 1:12 * NS + s], col(11, s - 1))
                    dve.reciprocal(col(12, s - 1), col(11, s - 1)).then_inc(rec_ready, 1)
                    dve.wait_ge(rec_ready, s)
                    wait(dve, olp_done, s - 1)
                    dve.tensor_scalar(fold_r[0:PW, :], fold[0:PW, :], smp[0:PW, 12 * NS + s - 1:12 * NS + s], None, ALU.mult).then_inc(foldr_ready, 1)
            dve.wait_ge(olp_done, NS)
            for c in range(KC):
                mm = dve.tensor_copy(olT[:, c, :, :], psum[:, 7, P + c * 64:P + (c + 1) * 64].rearrange("p (s h) -> p h s", s=NS))
            mm.then_inc(olT_ready, 1)
            split(U_O, U_O % STAGES, U_O % 2)
            split(U_O + 1, (U_O + 1) % STAGES, (U_O + 1) % 2)
            dve.wait_ge(os_done, 1)
            dve.tensor_copy(o[:, :, SEQ:T], psum[:, 0, 0:64].rearrange("p (h s) -> p h s", h=H)).then_inc(os_ready, 1)
            for g in range(0, 16, 2):
                dve.wait_ge(kv_done, g + 1)
                dst = kn[:, g, :] if g < 8 else v[:, (g - 8) // 2, 0:512]
                dve.tensor_copy(dst, psum[:, 4 + g % 4, :]).then_inc(kv_read_v, 1)

            for g in range(4 * H + 5):
                if g < 4 * H:
                    b = g % 4
                    n = (b + 1) * P
                    dve.wait_ge(s_done, g + 1)
                    dve.tensor_tensor(psum[:, g % 4, b * P:n], psum[:, g % 4, b * P:n], cmask, ALU.add).then_inc(s_masked, 1)
                    dve.wait_ge(s_masked, g + 1)
                    dve.tensor_reduce(small[:, 12 + g % 2:13 + g % 2], psum[:, g % 4, 0:n], AX_X, ALU.max).then_inc(s_max, 1)
                    dve.wait_ge(s_max, g + 1)
                    if g >= 2:
                        dve.wait_ge(p_exp, g - 1)
                    dve.tensor_scalar(small[:, 8 + g % 2:9 + g % 2], small[:, 12 + g % 2:13 + g % 2], -SCALE, None, ALU.mult).then_inc(s_neg, 1)
                if 1 <= g <= 4 * H:
                    e, n = g - 1, ((g - 1) % 4 + 1) * P
                    dve.wait_ge(p_exp, e + 1)
                    dve.reciprocal(small[:, 14 + e % 2:15 + e % 2], small[:, 10 + e % 2:11 + e % 2]).then_inc(p_rec, 1)
                    dve.wait_ge(p_rec, e + 1)
                    dve.tensor_scalar(pp[:, e % 2, 0:n], pp[:, e % 2, 0:n], small[:, 14 + e % 2:15 + e % 2], None, ALU.mult).then_inc(p_norm, 1)
                if g >= 8 and g % 4 == 0:
                    h = g // 4 - 2
                    dve.wait_ge(ov_done, h + 1)
                    dve.tensor_copy(o[:, h, 0:SEQ], psum[:, 6 + h % 2, :]).then_inc(o_ready, 1)
            for h in range(H):
                dve.wait_ge(oh_ready, h + 1)
                dve.wait_ge(o_ready, h + 1)
                dve.tensor_tensor(xl[:, h, :], o[:, h, :], f32(xh[:, h, :]), ALU.subtract).then_inc(ol_ready, 1)
            for t in range(KD):
                ahead_static(U_O + t)
                add_squares(dve, "m_attn", t, t % 2)
            update(3, m_attn)
            mlp(1)
            update(4, m_raw)
            for c in range(5):
                rows = P if c < 4 else NS
                dve.wait_ge(yT_done, c + 1)
                dve.tensor_copy(yn[0:rows, c, 0:512], psum[0:rows, 2 * (c % 2), :]).then_inc(y_ready_v, 1)


_INS = ["x_prompt", "x_sample", "cache_ckv", "cache_kr", "state_conv", "page_table", "pre_mix_g", "post_mix_g", "pre_ffn_g",
        "post_ffn_g", "w_in_a", "sgu_g", "w_s", "b_s", "w_out_a", "kv_in_g", "w_dkv", "kv_g", "w_uk", "w_uv", "w_dq", "q_g",
        "w_uq", "w_o", "w_up", "conv_w", "conv_b", "w_down"]
_OUTS = [("y_prompt", (1, SEQ, D)), ("y_sample", (NS, 1, D)), ("new_ckv_prompt", (1, SEQ, CL)), ("new_kr_prompt", (1, SEQ, ROPE)),
         ("new_conv_prompt", (DEPTH, 1, 2, 2 * DFF)), ("new_ckv_sample", (NS, 1, CL)), ("new_kr_sample", (NS, 1, ROPE)),
         ("new_conv_sample", (DEPTH, NS, 2, 2 * DFF)), ("new_chunkv_sample", (1, NS, 1, GW))]


def kernel(**inputs):
    import concourse.bacc as bacc
    from concourse.bass_utils import run_bass_kernel_spmd

    nc = bacc.Bacc("TRN2", target_bir_lowering=False, num_devices=1)
    arrays, a, outs = {}, {}, {}
    for name in _INS + ["consts"]:
        v = constants() if name == "consts" else np.ascontiguousarray(inputs[name])
        arrays[f"in_{name}"] = v
        a[name] = nc.dram_tensor(f"in_{name}", v.shape, mybir.dt.from_np(v.dtype), kind="ExternalInput").ap()
    for name, shape in _OUTS:
        outs[name] = nc.dram_tensor(f"out_{name}", shape, F32, kind="ExternalOutput").ap()
    trunk(nc, a, outs)
    r = run_bass_kernel_spmd(nc, [arrays], core_ids=[0])
    return tuple(r.results[0][f"out_{name}"] for name, _ in _OUTS)
```
